# Optimizing a Trainium2 kernel written in Bass

```python
import math
import jax
import jax.numpy as jnp
from jax import lax
import numpy as np

D_MODEL = 1024
BATCH = 1
SEQ = 128
DEPTH = 1
DEC_BATCH = 1
DEC_SEQ = 128
PAST_LEN = 128

GRID_W = 64
HEAD_DIM = 64
ATT_HEADS = 8
ATT_KV_HEADS = 2
ATT_WIDTH = ATT_HEADS * HEAD_DIM
KV_WIDTH = ATT_KV_HEADS * HEAD_DIM
RW_HEADS = 4
RW_WIDTH = RW_HEADS * HEAD_DIM
RW_DECAY_LORA = 64
RW_AAA_LORA = 64
RW_GATE_LORA = 128
RW_GN_EPS = 64e-5
HG_HEADS = 4
HG_WIDTH = HG_HEADS * HEAD_DIM
HG_CHUNK = 32
HG_F_MIN = 1e-6
MIX_WIDTH = ATT_WIDTH + RW_WIDTH + HG_WIDTH
IN_SIZES = (ATT_WIDTH, KV_WIDTH, KV_WIDTH, RW_WIDTH, RW_WIDTH, RW_WIDTH, 2 * RW_DECAY_LORA, 2 * RW_AAA_LORA, RW_GATE_LORA, HG_WIDTH, 2 * HG_WIDTH, HG_WIDTH, HG_WIDTH)
IN_WIDTH = ATT_WIDTH + 2 * KV_WIDTH + 3 * RW_WIDTH + 2 * RW_DECAY_LORA + 2 * RW_AAA_LORA + RW_GATE_LORA + 5 * HG_WIDTH
N_EXPERTS = 32
TOP_K = 4
EXPERT_FF = D_MODEL
SWIGLU_LIMIT = 7.0
SWIGLU_ALPHA = 1.702
MOE_BLOCK = 128
Q_BLOCK = 128
ROPE_THETA = 10000.0
NORM_EPS = 1e-6

kernel_name = 'hybrid_diffusion_attn_rwkv7_hgrn2_moe_step'

def rms_norm(x, g):
    xf = x.astype(jnp.float32)
    y = xf * lax.rsqrt(jnp.mean(xf * xf, axis=-1, keepdims=True) + NORM_EPS)
    return (y * g.astype(jnp.float32)).astype(x.dtype)

def axial_rope(n_tok):
    rows = n_tok // GRID_W
    row = jnp.repeat(jnp.arange(rows, dtype=jnp.float32), GRID_W)
    col = jnp.tile(jnp.arange(GRID_W, dtype=jnp.float32), rows)
    n_freq = HEAD_DIM // 4
    inv = ROPE_THETA ** (-jnp.arange(n_freq, dtype=jnp.float32) / n_freq)
    ang = jnp.concatenate([row[:, None] * inv, col[:, None] * inv], axis=-1)
    return jnp.cos(ang), jnp.sin(ang)

def apply_rope(x, cos, sin):
    xf = x.astype(jnp.float32).reshape(x.shape[:-1] + (HEAD_DIM // 2, 2))
    x1, x2 = xf[..., 0], xf[..., 1]
    out = jnp.stack([x1 * cos - x2 * sin, x1 * sin + x2 * cos], axis=-1)
    return out.reshape(x.shape).astype(x.dtype)

def block_attention(q, k, v):
    b, hq, tq, d = q.shape
    hkv = k.shape[1]
    rep = hq // hkv
    nblk = tq // Q_BLOCK
    qb = q.reshape(b, hkv, rep, nblk, Q_BLOCK, d).transpose(3, 0, 1, 2, 4, 5)
    scale = 1.0 / math.sqrt(d)

    def one_block(qblk):
        s = jnp.einsum('bgrqd,bgkd->bgrqk', qblk, k, preferred_element_type=jnp.float32) * scale
        pr = jax.nn.softmax(s, axis=-1)
        return jnp.einsum('bgrqk,bgkd->bgrqd', pr.astype(v.dtype), v)

    o = lax.map(one_block, qb)
    return o.transpose(1, 2, 3, 0, 4, 5).reshape(b, hq, tq, d)

def rwkv7_scan(r, w, k, v, a_, b_, s0):
    xs = tuple(jnp.moveaxis(t, 1, 0) for t in (r, w, k, v, a_, b_))

    def step(S, inp):
        rt, wt, kt, vt, at, bt = inp
        sa = jnp.einsum('bhvk,bhk->bhv', S, at)
        S = S * wt[:, :, None, :] + sa[..., None] * bt[:, :, None, :] + vt[..., None] * kt[:, :, None, :]
        return S, jnp.einsum('bhvk,bhk->bhv', S, rt)

    s_last, ys = lax.scan(step, s0, xs)
    return jnp.moveaxis(ys, 0, 1), s_last

def head_group_norm(y, g, b):
    mu = jnp.mean(y, axis=-1, keepdims=True)
    yc = y - mu
    var = jnp.mean(yc * yc, axis=-1, keepdims=True)
    yn = (yc * lax.rsqrt(var + RW_GN_EPS)).reshape(y.shape[0], y.shape[1], -1)
    return yn * g.astype(jnp.float32) + b.astype(jnp.float32)

def rwkv7_mixer(r, k, v, wd, ad, gd, p, s0):
    B, T, _ = r.shape
    f32 = jnp.float32
    heads = lambda t: t.astype(f32).reshape(B, T, RW_HEADS, HEAD_DIM)
    r, k, v = heads(r), heads(k), heads(v)
    wd = wd.astype(f32).reshape(B, T, 2, RW_DECAY_LORA)
    ad = ad.astype(f32).reshape(B, T, 2, RW_AAA_LORA)
    kk = k * p['rw_kk'].astype(f32).reshape(RW_HEADS, HEAD_DIM)
    kk = kk * lax.rsqrt(jnp.sum(kk * kk, axis=-1, keepdims=True) + 1e-12)
    g = jax.nn.sigmoid(gd.astype(f32)) @ p['rw_g2'].astype(f32)
    ka = p['rw_ka'].astype(f32).reshape(RW_HEADS, HEAD_DIM)
    rk = p['rw_rk'].astype(f32)
    ys, bonuses, states = [], [], []
    for d in range(2):
        w_raw = p['rw_w0'][d].astype(f32) + jnp.tanh(wd[:, :, d]) @ p['rw_w2'][d].astype(f32)
        decay = heads(jnp.exp(-jnp.exp(-jax.nn.softplus(-w_raw) - 0.5)))
        a = heads(jax.nn.sigmoid(p['rw_a0'][d].astype(f32) + ad[:, :, d] @ p['rw_a2'][d].astype(f32)))
        kd = k * (1.0 + (a - 1.0) * ka)
        seq = (r, decay, kd, v, -kk, kk * a)
        if d == 1:
            seq = tuple(jnp.flip(t, axis=1) for t in seq)
        y, s_last = rwkv7_scan(*seq, s0[:, d].astype(f32))
        if d == 1:
            y = jnp.flip(y, axis=1)
        ys.append(y)
        bonuses.append(jnp.sum(r * kd * rk, axis=-1, keepdims=True) * v)
        states.append(s_last)
    y = head_group_norm(ys[0] + ys[1], p['rw_gn_g'], p['rw_gn_b']) + (bonuses[0] + bonuses[1]).reshape(B, T, RW_WIDTH)
    return y * g, jnp.stack(states, axis=1)

def chunk_gla(q, k, v, logf, s0):
    B, H, T, dk = q.shape
    dv = v.shape[-1]
    n = T // HG_CHUNK
    rs = lambda t: t.reshape(B, H, n, HG_CHUNK, t.shape[-1])
    q, k, v, logf = rs(q), rs(k), rs(v), rs(logf)
    b = jnp.cumsum(logf, axis=3)
    causal = jnp.tril(jnp.ones((HG_CHUNK, HG_CHUNK), dtype=bool))
    diff = b[:, :, :, :, None, :] - b[:, :, :, None, :, :]
    dec = jnp.where(causal[:, :, None], jnp.exp(jnp.minimum(diff, 0.0)), 0.0)
    att = jnp.einsum('bhntd,bhnsd,bhntsd->bhnts', q, k, dec)
    o_intra = jnp.einsum('bhnts,bhnsv->bhntv', att, v)
    b_last = b[:, :, :, -1, :]
    kv = jnp.einsum('bhnsd,bhnsv->bhndv', k * jnp.exp(b_last[:, :, :, None, :] - b), v)

    def step(S, inp):
        dl, kvn = inp
        return dl[..., None] * S + kvn, S

    s_last, s_before = lax.scan(step, s0, (jnp.moveaxis(jnp.exp(b_last), 2, 0), jnp.moveaxis(kv, 2, 0)))
    s_before = jnp.moveaxis(s_before, 0, 2)
    o_inter = jnp.einsum('bhntd,bhndv->bhntv', q * jnp.exp(b), s_before)
    return (o_intra + o_inter).reshape(B, H, T, dv), s_last

def hgrn2_mixer(q, f_raw, i, g, lb, norm_g, s0):
    B, T, _ = q.shape
    f32 = jnp.float32
    heads = lambda t: t.astype(f32).reshape(B, T, HG_HEADS, HEAD_DIM).transpose(0, 2, 1, 3)
    qh = heads(jax.nn.silu(q.astype(f32)))
    vh = heads(i)
    f_raw = f_raw.astype(f32).reshape(B, T, 2, HG_WIDTH)
    outs, states = [], []
    for d in range(2):
        lbd = lb[d]
        f = lbd + (1.0 - lbd) * jax.nn.sigmoid(f_raw[:, :, d])
        logf = jnp.log(jnp.maximum(f, HG_F_MIN))
        kf = 1.0 - f
        seq = (qh, heads(kf), vh, heads(logf))
        if d == 1:
            seq = tuple(jnp.flip(t, axis=2) for t in seq)
        o, s_last = chunk_gla(*seq, s0[:, d].astype(f32))
        if d == 1:
            o = jnp.flip(o, axis=2)
        outs.append(o)
        states.append(s_last)
    o = rms_norm(outs[0] + outs[1], norm_g).transpose(0, 2, 1, 3).reshape(B, T, HG_WIDTH)
    return o * jax.nn.silu(g.astype(f32)), jnp.stack(states, axis=1)

def moe(h, p):
    T, D = h.shape
    logits = (h @ p['router_w']).astype(jnp.float32) + p['router_b'].astype(jnp.float32)
    top_logit, top_idx = lax.top_k(logits, TOP_K)
    gates = jax.nn.softmax(top_logit, axis=-1)
    A = T * TOP_K
    flat_e = top_idx.reshape(A)
    flat_tok = jnp.arange(A, dtype=jnp.int32) // TOP_K
    flat_g = gates.reshape(A)
    order = jnp.argsort(flat_e)
    se = flat_e[order]
    counts = jnp.bincount(flat_e, length=N_EXPERTS)
    starts = jnp.cumsum(counts) - counts
    padded = (counts + MOE_BLOCK - 1) // MOE_BLOCK * MOE_BLOCK
    pends = jnp.cumsum(padded)
    pstarts = pends - padded
    dest = pstarts[se] + jnp.arange(A, dtype=jnp.int32) - starts[se]
    n_blocks = -(-(A + N_EXPERTS * (MOE_BLOCK - 1)) // MOE_BLOCK)
    n_slots = n_blocks * MOE_BLOCK
    slot_tok = jnp.full((n_slots,), T, dtype=jnp.int32).at[dest].set(flat_tok[order])
    slot_g = jnp.zeros((n_slots,), dtype=jnp.float32).at[dest].set(flat_g[order])
    block_e = jnp.clip(jnp.searchsorted(pends, jnp.arange(n_blocks, dtype=jnp.int32) * MOE_BLOCK, side='right'), 0, N_EXPERTS - 1)
    h_pad = jnp.concatenate([h, jnp.zeros((1, D), h.dtype)], axis=0)
    xb = h_pad[slot_tok].reshape(n_blocks, MOE_BLOCK, D)

    def expert_block(args):
        xblk, e = args
        gu = xblk @ p['moe_w_gu'][e] + p['moe_b_gu'][e]
        glu, lin = gu[:, :EXPERT_FF], gu[:, EXPERT_FF:]
        glu = jnp.minimum(glu, SWIGLU_LIMIT)
        lin = jnp.clip(lin, -SWIGLU_LIMIT, SWIGLU_LIMIT)
        act = glu * jax.nn.sigmoid(SWIGLU_ALPHA * glu) * (lin + 1.0)
        return act @ p['moe_w_down'][e] + p['moe_b_down'][e]

    yb = lax.map(expert_block, (xb, block_e)).reshape(n_slots, D)
    y = jax.ops.segment_sum(yb * slot_g[:, None].astype(yb.dtype), slot_tok, num_segments=T + 1)[:T]
    return y.astype(h.dtype)

def token_mixers(h, p, lb, cache):
    B, T, _ = h.shape
    proj = h @ p['w_in']
    split_points = np.cumsum(IN_SIZES)[:-1].tolist()
    (aq, ak, av, rr, rk, rv, rwd, rad, rgd, hq, hf, hi, hg) = jnp.split(proj, split_points, axis=-1)
    qh = rms_norm(aq.reshape(B, T, ATT_HEADS, HEAD_DIM), p['att_qnorm_g']).transpose(0, 2, 1, 3)
    kh = rms_norm(ak.reshape(B, T, ATT_KV_HEADS, HEAD_DIM), p['att_knorm_g']).transpose(0, 2, 1, 3)
    vh = av.reshape(B, T, ATT_KV_HEADS, HEAD_DIM).transpose(0, 2, 1, 3)
    if cache is None:
        att = block_attention(qh, kh, vh)
        rw_s0 = jnp.zeros((B, 2, RW_HEADS, HEAD_DIM, HEAD_DIM), jnp.float32)
        hg_s0 = jnp.zeros((B, 2, HG_HEADS, HEAD_DIM, HEAD_DIM), jnp.float32)
    else:
        ck, cv, rw_s0, hg_s0 = cache
        cos, sin = axial_rope(T)
        qr = apply_rope(qh, cos, sin)
        kr = apply_rope(kh, cos, sin)
        att = block_attention(qr, jnp.concatenate([ck.astype(kr.dtype), kr], axis=2), jnp.concatenate([cv.astype(vh.dtype), vh], axis=2))
    att = att.transpose(0, 2, 1, 3).reshape(B, T, ATT_WIDTH)
    rw_out, rw_state = rwkv7_mixer(rr, rk, rv, rwd, rad, rgd, p, rw_s0)
    hg_out, hg_state = hgrn2_mixer(hq, hf, hi, hg, lb, p['hg_norm_g'], hg_s0)
    mix = jnp.concatenate([att.astype(h.dtype), rw_out.astype(h.dtype), hg_out.astype(h.dtype)], axis=-1)
    new_cache = (kh, vh, rw_state, hg_state) if cache is None else None
    return mix, new_cache

def layer(x, mod, p, lb, cache):
    shift1, scale1, gate1, shift2, scale2, gate2 = jnp.split(mod[:, None, :], 6, axis=-1)
    h = rms_norm(x, p['norm_mix_g']) * (1.0 + scale1) + shift1
    mix, new_cache = token_mixers(h, p, lb, cache)
    x = x + gate1 * (mix @ p['w_out'])
    h = rms_norm(x, p['norm_ffn_g']) * (1.0 + scale2) + shift2
    B, T, D = h.shape
    x = x + gate2 * moe(h.reshape(B * T, D), p).reshape(B, T, D)
    return x, new_cache

def hgrn_lower_bounds(hg_lb):
    sm = jax.nn.softmax(hg_lb.astype(jnp.float32), axis=0)
    return jnp.cumsum(sm, axis=0) - sm[0:1]

def setup_inputs(seed: int = 0) -> dict:
    key = jax.random.key(seed)
    kit = iter(jax.random.split(key, 40))
    nrm = lambda shape, scale: scale * jax.random.normal(next(kit), shape, jnp.float32)
    gain = lambda shape: 1.0 + nrm(shape, 0.02)
    D = D_MODEL
    return {
        'x_prompt': nrm((BATCH, SEQ, D), 1.0),
        'x_sample': nrm((DEC_BATCH, DEC_SEQ, D), 1.0),
        'cache_att_k': nrm((DEC_BATCH, DEPTH, ATT_KV_HEADS, PAST_LEN, HEAD_DIM), 1.0),
        'cache_att_v': nrm((DEC_BATCH, DEPTH, ATT_KV_HEADS, PAST_LEN, HEAD_DIM), 1.0),
        'state_rwkv': nrm((DEC_BATCH, DEPTH, 2, RW_HEADS, HEAD_DIM, HEAD_DIM), 0.5),
        'state_hgrn': nrm((DEC_BATCH, DEPTH, 2, HG_HEADS, HEAD_DIM, HEAD_DIM), 0.5),
        'c': nrm((DEC_BATCH, D), 1.0),
        'c_ctx': nrm((D,), 1.0),
        'w_mod': nrm((DEPTH, D, 6 * D), 0.5 * D ** -0.5),
        'b_mod': nrm((DEPTH, 6 * D), 0.02),
        'norm_mix_g': gain((DEPTH, D)),
        'norm_ffn_g': gain((DEPTH, D)),
        'w_in': nrm((DEPTH, D, IN_WIDTH), D ** -0.5),
        'w_out': nrm((DEPTH, MIX_WIDTH, D), MIX_WIDTH ** -0.5),
        'att_qnorm_g': gain((DEPTH, HEAD_DIM)),
        'att_knorm_g': gain((DEPTH, HEAD_DIM)),
        'rw_w0': nrm((DEPTH, 2, RW_WIDTH), 0.5),
        'rw_w2': nrm((DEPTH, 2, RW_DECAY_LORA, RW_WIDTH), 0.5 * RW_DECAY_LORA ** -0.5),
        'rw_a0': nrm((DEPTH, 2, RW_WIDTH), 0.5),
        'rw_a2': nrm((DEPTH, 2, RW_AAA_LORA, RW_WIDTH), 0.5 * RW_AAA_LORA ** -0.5),
        'rw_g2': nrm((DEPTH, RW_GATE_LORA, RW_WIDTH), RW_GATE_LORA ** -0.5),
        'rw_kk': 0.85 + nrm((DEPTH, RW_WIDTH), 0.05),
        'rw_ka': 1.0 + nrm((DEPTH, RW_WIDTH), 0.05),
        'rw_rk': nrm((DEPTH, RW_HEADS, HEAD_DIM), 0.1),
        'rw_gn_g': gain((DEPTH, RW_WIDTH)),
        'rw_gn_b': nrm((DEPTH, RW_WIDTH), 0.02),
        'hg_lb': nrm((DEPTH, 2, HG_WIDTH), 1.0),
        'hg_norm_g': gain((DEPTH, HEAD_DIM)),
        'router_w': nrm((DEPTH, D, N_EXPERTS), D ** -0.5),
        'router_b': nrm((DEPTH, N_EXPERTS), 0.01),
        'moe_w_gu': nrm((DEPTH, N_EXPERTS, D, 2 * EXPERT_FF), D ** -0.5),
        'moe_b_gu': nrm((DEPTH, N_EXPERTS, 2 * EXPERT_FF), 0.02),
        'moe_w_down': nrm((DEPTH, N_EXPERTS, EXPERT_FF, D), EXPERT_FF ** -0.5),
        'moe_b_down': nrm((DEPTH, N_EXPERTS, D), 0.02),
        'final_norm_g': gain((D,)),
    }

def reference(x_prompt, x_sample, cache_att_k, cache_att_v, state_rwkv, state_hgrn, c, c_ctx,
              w_mod, b_mod, norm_mix_g, norm_ffn_g, w_in, w_out, att_qnorm_g, att_knorm_g,
              rw_w0, rw_w2, rw_a0, rw_a2, rw_g2, rw_kk, rw_ka, rw_rk, rw_gn_g, rw_gn_b,
              hg_lb, hg_norm_g, router_w, router_b, moe_w_gu, moe_b_gu, moe_w_down, moe_b_down,
              final_norm_g):
    lb_all = hgrn_lower_bounds(hg_lb)
    silu_ctx = jax.nn.silu(c_ctx)[None, :]
    silu_lat = jax.nn.silu(c)
    xp, xs = x_prompt, x_sample
    ks, vs, srs, shs = [], [], [], []
    for l in range(DEPTH):
        p = dict(norm_mix_g=norm_mix_g[l], norm_ffn_g=norm_ffn_g[l], w_in=w_in[l], w_out=w_out[l],
                 att_qnorm_g=att_qnorm_g[l], att_knorm_g=att_knorm_g[l],
                 rw_w0=rw_w0[l], rw_w2=rw_w2[l], rw_a0=rw_a0[l], rw_a2=rw_a2[l], rw_g2=rw_g2[l],
                 rw_kk=rw_kk[l], rw_ka=rw_ka[l], rw_rk=rw_rk[l], rw_gn_g=rw_gn_g[l], rw_gn_b=rw_gn_b[l],
                 hg_norm_g=hg_norm_g[l], router_w=router_w[l], router_b=router_b[l],
                 moe_w_gu=moe_w_gu[l], moe_b_gu=moe_b_gu[l], moe_w_down=moe_w_down[l], moe_b_down=moe_b_down[l])
        xp, (k_l, v_l, sr_l, sh_l) = layer(xp, silu_ctx @ w_mod[l] + b_mod[l], p, lb_all[l], None)
        ks.append(k_l)
        vs.append(v_l)
        srs.append(sr_l)
        shs.append(sh_l)
        xs, _ = layer(xs, silu_lat @ w_mod[l] + b_mod[l], p, lb_all[l],
                      (cache_att_k[:, l], cache_att_v[:, l], state_rwkv[:, l], state_hgrn[:, l]))
    y_prompt = rms_norm(xp, final_norm_g)
    y_sample = rms_norm(xs, final_norm_g)
    new_att_k = jnp.stack(ks, axis=1)
    new_att_v = jnp.stack(vs, axis=1)
    new_state_rwkv = jnp.stack(srs, axis=1)
    new_state_hgrn = jnp.stack(shs, axis=1)
    return (y_prompt, y_sample, new_att_k, new_att_v, new_state_rwkv, new_state_hgrn)


_drawn_inputs = setup_inputs


def setup_inputs(seed=0):
    import zlib

    import numpy as np

    out = dict(_drawn_inputs(seed))
    spreads = {}
    factors = {'cache_att_k': 3.01,
     'cache_att_v': 2.849,
     'state_rwkv': 8.0,
     'state_hgrn': 8.0,
     'norm_ffn_g': 3.134,
     'att_qnorm_g': 8.0,
     'att_knorm_g': 3.037,
     'rw_kk': 17.895,
     'rw_gn_g': 7.201,
     'rw_gn_b': 8.0,
     'hg_norm_g': 8.0,
     'router_b': 5.328,
     'moe_b_gu': 8.0,
     'moe_b_down': 29.284,
     'final_norm_g': 7.897}
    for name, (base, spread) in spreads.items():
        noise = np.random.default_rng([zlib.crc32(name.encode()), seed]).standard_normal(out[name].shape)
        drawn = base * np.exp(spread * noise) if base else spread * noise
        out[name] = jnp.asarray(drawn.astype(out[name].dtype))
    for name, factor in factors.items():
        out[name] = (out[name] * factor).astype(out[name].dtype)
    return out
```

```python
from contextlib import ExitStack
import math

import numpy as np
import concourse.bass as bass
from concourse import mybir

F32 = mybir.dt.float32
I32 = mybir.dt.int32
U32 = mybir.dt.uint32
ALU = mybir.AluOpType
ACT = mybir.ActivationFunctionType
AX = mybir.AxisListType

P = 128
D = 1024
KC = D // P
DH = 64
FF = 1024
NE = 32
TOPK = 4
CAP = 64
NBATCH = 2 * P // CAP
EPS = 1e-6
GN_EPS = 64e-5
DECAY = math.exp(-0.5)
ALPHA, LIMIT = 1.702, 7.0

AQ, AK, AV, RR, RK, RV, RWD, RAD, RGD, HQ, HF, HI, HG, IN_W = (
    0, 512, 640, 768, 1024, 1280, 1536, 1664, 1792, 1920, 2176, 2688, 2944, 3200)
PIECES = [(768, 512), (1280, 512), (1792, 512), (2304, 512), (2816, 384), (0, 512), (512, 256)]

SLOT = 4096
NSLOT = 6
FRONT_SLOTS = 3
FRONT_RING = [(0, 1, 2, NSLOT - 1)[i % 4] for i in range(4 + len(PIECES) + 4 + 4)] + [0, 1]
FRONT_ROUNDS = [FRONT_RING.count(j) for j in range(NSLOT)]

LEVELS = [64, 32, 16, 8]
DIAG = 8


def layout(items):
    at, out = 0, {}
    for name, n in items:
        out[name] = (at, at + n)
        at += n
    return out, at


CONST, CONST_W = layout([
    ("ident", P), ("cent0", P), ("excl0", P), ("cent1", P), ("excl1", P), ("halves0", 2), ("halves1", 2),
    ("hg0", 6 * P), ("hg1", 6 * P), ("after0", P), ("after1", P),
    ("merge0", 7 * P), ("merge1", 7 * P), ("diag0", P), ("diag1", P),
    ("tri0", 2 * P), ("tri1", 2 * P), ("sel", 8 * P), ("ones", P), ("iota", (NBATCH + 1) * P), ("iota_e", NE),
    ("cos", 32), ("sin", 32)])

PARAM, PARAM_W = layout([
    ("fin_g", D), ("w0", 512), ("a0", 512), ("kk", 256), ("ka", 256), ("rk", 256), ("gn_g", 256), ("gn_b", 256),
    ("lb", 512), ("q_g", DH), ("k_g", DH), ("hg_g", DH), ("router_b", NE), ("ffn_g", D)])


def constants():
    c = np.zeros((P, CONST_W), np.float32)

    def put(name, a):
        lo, hi = CONST[name]
        c[:, lo:hi] = a.reshape(a.shape[0], -1)

    r, t = np.arange(P)[:, None], np.arange(P)[None, :]
    put("ident", (r == t) * 1.0)
    for d in range(2):
        before = (r < t) if d == 0 else (r > t)
        upto = before | (r == t)
        first = ((r < 64) if d == 0 else (r >= 64)) * np.ones((1, P), bool)
        put(f"cent{d}", upto * 1.0 - first)
        put(f"excl{d}", before * 1.0 - first)
        put(f"halves{d}", np.concatenate([first[:, :1], ~first[:, :1]], 1) * 1.0)
        pr, pt = (r, t) if d == 0 else (P - 1 - r, P - 1 - t)
        mats = []
        for m in LEVELS:
            mid = pt // (2 * m) * (2 * m) + m
            mats.append(np.where(pt >= mid, (pr >= mid) & (pr <= pt), (pr > pt) & (pr < mid)) * 1.0)
        mid = pt // DIAG * DIAG + DIAG // 2
        mats.append(((pr >= mid) & (pr <= pt)) * 1.0 - ((pr > pt) & (pr < mid)) * 1.0)
        mats.append(upto * 1.0)
        put(f"hg{d}", np.concatenate(mats, 1))
        put(f"after{d}", (pr > pt) * 1.0)
        merge = []
        for k in range(7):
            m = 1 << k
            merge.append(((pr // (2 * m) == pt // (2 * m)) & (pr % (2 * m) < m) & (pt % (2 * m) >= m)) * 1.0)
        put(f"merge{d}", np.concatenate(merge, 1))
        put(f"diag{d}", ((pr // DIAG == pt // DIAG) & (pr <= pt)) * 1.0)
        put(f"tri{d}", np.concatenate([before * 1.0, upto * 1.0], 1))
    sel = np.zeros((P, 4, 2, P), np.float32)
    for q in range(4):
        for s in range(2):
            sel[32 * q + s, q, s, :] = 1.0
    put("sel", sel)
    put("ones", np.ones((P, P)))
    io = np.stack([np.concatenate([np.arange(CAP), np.arange(CAP)]) + b * CAP for b in range(NBATCH + 1)])
    put("iota", np.broadcast_to(io[None], (P, NBATCH + 1, P)))
    put("iota_e", np.broadcast_to(np.arange(NE)[None], (P, NE)))
    tok = np.arange(P)
    inv = 10000.0 ** (-np.arange(16, dtype=np.float64) / 16)
    ang = np.concatenate([(tok // 64)[:, None] * inv, (tok % 64)[:, None] * inv], 1)
    put("cos", np.cos(ang))
    put("sin", np.sin(ang))
    return c


def psum_jobs():
    jobs = [("mod", 0), ("modT",)]
    jobs += [("xT", s, h) for s in range(2) for h in range(2)]
    for n in range(len(PIECES)):
        jobs += [("proj", n, s) for s in range(2)] + ([("mod", 1 + n // 2)] if n in (0, 2) else [])
    for s in range(2):
        jobs += [("rw_loraT", s), ("rw_wa", s, 0), ("rw_wa", s, 1), ("rw_g", s)]
        jobs += [("hg_T", s, 0), ("hg_T", s, 1)]
        jobs += [("hg_E", s, d, p, x) for d in range(2) for p in range(2) for x in range(2)]
        jobs += [("rw_cum", s, 0), ("rw_cum", s, 1), ("rw_half", s)]
        jobs += [("rw_s0T", s)] if s else []
        jobs += [("rw_T", s, d, x) for d in range(2) for x in range(2)]
        jobs += [("hg_att", s, d, q, l) for d in range(2) for q in range(2) for l in range(3)]
        jobs += [(n, s, d, q) for d in range(2) for n in ("rw_b", "rw_k", "rw_L") for q in range(2)]
        jobs += [("hg_o", s)]
        jobs += [("hg_after", s), ("hg_st", s)] if s == 0 else []
        for k in range(1, 7):
            jobs += [(n, s, k, d) for n in ("rw_W", "rw_X", "rw_Y") for d in range(2) if (n, k) != ("rw_X", 6)]
        jobs += [("rw_R", s, d) for d in range(2)] + [("rw_u", s, d) for d in range(2)] + [("rw_y", s)]
        jobs += [("rw_st", s), ("rw_stT", s)] if s == 0 else []
    for s in range(2):
        nk = 1 + s
        jobs += [("at_qT", s), ("at_kT", s)]
        jobs += [("at_S", s, i) for i in range(2 * nk)]
        jobs += [("bc", v, t, h) for v in ((0,), (1, 2))[s] for t in range(2) for h in range(2)]
        jobs += [("at_PT", s, i) for i in range(2 * nk)] + [("at_o", s)]
    jobs += [("mixT", s, h) for s in range(2) for h in range(2)]
    jobs += [("out", s, h) for s in range(2) for h in range(2)]
    jobs += [("bc", 3, s, h) for s in range(2) for h in range(2)]
    jobs += [("h2T", s, h) for s in range(2) for h in range(2)]
    jobs += [("router",), ("pos",)]
    return {name: k for k, name in enumerate(jobs)}


def build(nc, a):
    jobs = psum_jobs()
    with ExitStack() as ctx:
        def sb(name, shape, dt=F32):
            return ctx.enter_context(nc.sbuf_tensor(name, shape, dt))

        sems = {}

        def sem(name):
            if name not in sems:
                sems[name] = ctx.enter_context(nc.semaphore(name))
            return sems[name]

        ring = sb("ring", [P, NSLOT, SLOT])
        const = sb("const_sb", [P, CONST_W])
        param = sb("param_sb", [P, PARAM_W])
        proj = sb("proj", [P, 2, IN_W])
        hT_t = sb("hT", [P, 2 * D])
        h_t = sb("h_nat", [P, 2 * D])
        mix = sb("mix", [P, 2, D])
        x = sb("x_res", [P, 2, D])
        mod_sb = sb("mod_sb", [P, 3, 512])
        small = sb("small", [P, 256])
        router_w = sb("router_w_sb", [P, KC, NE])
        bank = [ctx.enter_context(nc.psum_tensor(f"bank{i}", [P, 512], F32)) for i in range(8)]

        hT = hT_t[:, :].rearrange("p (s c t) -> p s c t", s=2, c=KC)
        h = h_t[:, :].rearrange("p (s n) -> p s n", s=2)
        scratch = ring[:, FRONT_SLOTS:, :].rearrange("p a b -> p (a b)")

        def C(name):
            lo, hi = CONST[name]
            return const[:, lo:hi]

        def Pm(name):
            lo, hi = PARAM[name]
            return param[:, lo:hi]

        ident, ones = C("ident"), C("ones")

        def carve(base, items):
            offs, w = layout(items)
            assert w <= base.shape[1], (w, base.shape)
            return {n: base[:, lo:hi] for n, (lo, hi) in offs.items()}

        keep = carve(scratch, [("w2", 256), ("a2", 256), ("g2", 256), ("ck", P), ("cv", P), ("rw_st", 512), ("hg_st", 512), ("c_silu", 256),
                               ("s0", 512)])
        temp = scratch[:, 2816:]
        early = carve(temp[:, 0:2 * SLOT - 2816], [("c", 256), ("csig", 256), ("g_col", KC), ("sq", D),
                             ("modT", 512), ("s1", 2 * KC)])
        rw = carve(temp, [("th", 256), ("loraT", 384), ("kk", 256), ("W", 1024), ("sa", 1024), ("g", 256),
                          ("X", 1024), ("TL", 2048), ("AK", 2048), ("Y", 1024)])
        front = ring[:, 0:FRONT_SLOTS, :].rearrange("p a b -> p (a b)")
        hg = carve(front, [("q", 256), ("gg", 256), ("fs", 512), ("kf", 512), ("logf", 512), ("qT", 256), ("kT", 512),
                          ("qL", 3072), ("kL", 2560), ("E", 1792), ("att", 1024), ("kh", 512), ("st", 256)])
        hg_att, hg_E = hg, hg["E"]
        at = carve(temp, [("sq", 640), ("qn", 640), ("rope", 640), ("t1", 320), ("t2", 320), ("t3", 320), ("t4", 320),
                          ("qT", 512), ("kT", 256), ("S", 2048), ("PT", 2048)])

        flat = proj[:, :, :].rearrange("p s n -> p (s n)")
        gate1, scale2, shift2 = proj[:, :, RR:RR + D], proj[:, :, RR + D:RR + 2 * D], h
        moe = carve(flat, [("xe", 512), ("xeT", 512), ("glu", 512), ("sig", 512), ("lin", 512), ("act", 512),
                           ("actT", 512), ("y", 512), ("hot", 2 * CAP), ("hotg", 2 * P), ("scat", 2 * P), ("zero", 512)])
        gate2 = mix
        bias_row = param[0:1, D:D + 3 * D]
        sel_e = carve(small[:, :], [("pos", 2 * NE), ("gate", 2 * NE), ("m8", 16), ("e4", 8), ("a", 16), ("b", 16), ("c", 16),
                                    ("idxf", 8), ("d", 16), ("cnt", 1), ("cnt_i", 1), ("idx8", 16)])
        idx8 = sel_e["idx8"].bitcast(U32).rearrange("p (s k) -> p s k", s=2)
        count_i = sel_e["cnt_i"].bitcast(I32)
        one8 = hT_t[:, 0:2 * TOPK * NE].rearrange("p (s k e) -> p s k e", s=2, k=TOPK)
        logits = hT_t[:, 512:512 + 2 * NE].rearrange("p (s e) -> p s e", s=2)
        selm = hT_t[:, 640:640 + 2 * NE].rearrange("p (s e) -> p s e", s=2)
        tmp_e = hT_t[:, 768:768 + 2 * TOPK * NE].rearrange("p (s k e) -> p s k e", s=2, k=TOPK)
        pos = sel_e["pos"].rearrange("p (s e) -> p s e", s=2)
        gate = sel_e["gate"].rearrange("p (s e) -> p s e", s=2)

        full = [sem(f"bank_full{i}") for i in range(8)]
        free = [sem(f"bank_free{i}") for i in range(8)]
        ring_full = [sem(f"ring_full{i}") for i in range(NSLOT)]
        ring_used = [sem(f"ring_used{i}") for i in range(NSLOT)]
        phase = sem("phase")

        def open_bank(pe, *name):
            k = jobs[name]
            if k >= 8:
                pe.wait_ge(free[k % 8], k // 8)
            return bank[k % 8]

        def filled(ins, *name):
            ins.then_inc(full[jobs[name] % 8], 1)

        def take(eng, *name):
            k = jobs[name]
            eng.wait_ge(full[k % 8], k // 8 + 1)
            return bank[k % 8]

        def done(ins, *name):
            ins.then_inc(free[jobs[name] % 8], 1)

        class Steps:

            def __init__(self, eng, name):
                self.eng, self.sem, self.n = eng, sem(name), 0

            def __call__(self, ins):
                ins.then_inc(self.sem, 1)
                self.n += 1
                self.eng.wait_ge(self.sem, self.n)

        def end_phase(eng, k):
            eng.drain().then_inc(phase, 1)
            eng.wait_ge(phase, 3 * (k + 1))

        def bc(ap, shape, *axes):
            for ax in axes:
                ap = ap.unsqueeze(ax)
            return ap.to_broadcast(shape)

        PH_EARLY, PH_MIX, PH_AT, PH_MID, PH_ROUTE = 0, 1, 3, 5, 6

        block = ctx.enter_context(nc.Block())

        w_mod = a["w_mod"][0].rearrange("(c p) n -> p c n", p=P)
        w_in = a["w_in"][0].rearrange("(c p) n -> p c n", p=P)
        w_out = a["w_out"][0].rearrange("(c p) n -> p c n", p=P)

        @block.sync
        def _(sp):
            def ring_load(i, src, width):
                s = FRONT_RING[i]
                if FRONT_RING[:i].count(s):
                    sp.wait_ge(ring_used[s], FRONT_RING[:i].count(s))
                n = src.shape[1] * width
                sp.dma_start(ring[:, s, 0:n].rearrange("p (c n) -> p c n", n=width), src).then_inc(ring_full[s], 16)

            i = 0

            def mod_loads(g, js, i):
                for j in js:
                    ring_load(i, w_mod[:, 2 * j:2 * j + 2, 2048 * g:2048 * (g + 1)], 2048)
                    i += 1
                return i

            i = mod_loads(0, range(4), i)
            for n, (lo, w) in enumerate(PIECES):
                ring_load(i, w_in[:, :, lo:lo + w], w)
                i += 1
                if n < 4:
                    i = mod_loads(1 + n // 2, range(2 * (n % 2), 2 * (n % 2) + 2), i)
            sp.wait_ge(phase, 3 * PH_AT)
            sp.wait_ge(sem("hg_out"), 16)
            for j in range(2):
                ring_load(i, w_out[:, 4 * j:4 * j + 4, :], D)
                i += 1

            def expert_load(e, j):
                wgu = a["moe_w_gu"][0, bass.ds(e, 1)].rearrange("e (c p) n -> p (e c) n", p=P) if not isinstance(e, int) \
                    else a["moe_w_gu"][0, e].rearrange("(c p) n -> p c n", p=P)
                wdn = a["moe_w_down"][0, bass.ds(e, 1)].rearrange("e (c p) n -> p (e c) n", p=P) if not isinstance(e, int) \
                    else a["moe_w_down"][0, e].rearrange("(c p) n -> p c n", p=P)
                src = wgu[:, 2 * j:2 * j + 2, :] if j < 4 else wdn[:, 4 * (j - 4):4 * (j - 4) + 4, :]
                w = 2048 if j < 4 else D
                sp.dma_start(ring[:, j, :].rearrange("p (c n) -> p c n", n=w), src).then_inc(ring_full[j], 16)

            for j in range(NSLOT):
                if FRONT_ROUNDS[j]:
                    sp.wait_ge(ring_used[j], FRONT_ROUNDS[j])
                if j == FRONT_SLOTS:
                    sp.wait_ge(phase, 3 * PH_MID)
                    sp.wait_ge(sem("cache_out"), 16 * 2)
                expert_load(0, j)
            with sp.Fori(1, NE) as e:
                for j in range(NSLOT):
                    sp.wait_ge(ring_used[j], e + FRONT_ROUNDS[j])
                    expert_load(e, j)
            sp.wait_ge(sem("counted"), 1)
            need = sp.value_load(count_i[0:1, 0:1])
            with sp.If(need > CAP):
                with sp.Fori(1, NBATCH) as b:
                    with sp.Fori(0, NE) as e:
                        for j in range(NSLOT):
                            sp.wait_ge(ring_used[j], b * NE + e + FRONT_ROUNDS[j])
                            expert_load(e, j)
            sp.wait_ge(sem("y_ready"), 2)
            for s, name in enumerate(("y_prompt", "y_sample")):
                sp.dma_start(a[name][0], h[:, s, :]).then_inc(sem("y_out"), 16)
            sp.wait_ge(sem("y_out"), 32)

        @block.gpsimd
        def _(pool):
            pool.dma_start(x[:, 0, :], a["x_prompt"][0]).then_inc(sem("x_in"), 16)
            pool.dma_start(x[:, 1, :], a["x_sample"][0]).then_inc(sem("x_in"), 16)
            pool.dma_start(const[:, :], a["constants"]).then_inc(sem("const_in"), 16)
            pool.dma_start(early["g_col"], a["norm_mix_g"][0].rearrange("(c p) -> p c", p=P),
                           allow_slow_non_contiguous=True).then_inc(sem("gcol_in"), 16)
            pool.wait_ge(sem("zeroed"), 1)
            bsrc = a["b_mod"][0].rearrange("(g q n) -> q g n", g=3, q=4)
            for s in range(2):
                pool.dma_start(mod_sb[s:s + 97:32], bsrc).then_inc(sem("bmod_in"), 16)
            for name, src in (
                    ("w0", a["rw_w0"][0].rearrange("d n -> (d n)")), ("a0", a["rw_a0"][0].rearrange("d n -> (d n)")),
                    ("kk", a["rw_kk"][0]), ("ka", a["rw_ka"][0]), ("rk", a["rw_rk"][0].rearrange("h d -> (h d)")),
                    ("gn_g", a["rw_gn_g"][0]), ("gn_b", a["rw_gn_b"][0]), ("lb", a["hg_lb"][0].rearrange("d n -> (d n)")),
                    ("q_g", a["att_qnorm_g"][0]), ("k_g", a["att_knorm_g"][0]), ("hg_g", a["hg_norm_g"][0]),
                    ("router_b", a["router_b"][0]), ("ffn_g", a["norm_ffn_g"][0]), ("fin_g", a["final_norm_g"])):
                n = src.shape[0]
                pool.dma_start(Pm(name), src.unsqueeze(0).to_broadcast([P, n])).then_inc(sem("param_in"), 16)
            pool.dma_start(keep["w2"], a["rw_w2"][0].rearrange("d r n -> (d r) n")).then_inc(sem("mixer_in"), 16)
            pool.dma_start(keep["a2"], a["rw_a2"][0].rearrange("d r n -> (d r) n")).then_inc(sem("mixer_in"), 16)
            pool.dma_start(keep["g2"], a["rw_g2"][0]).then_inc(sem("mixer_in"), 16)
            pool.dma_start(keep["ck"].rearrange("k (g d) -> k g d", g=2), a["cache_att_k"][0, 0].rearrange("g k d -> k g d")) \
                .then_inc(sem("mixer_in"), 16)
            pool.dma_start(keep["cv"].rearrange("k (g d) -> k g d", g=2), a["cache_att_v"][0, 0].rearrange("g k d -> k g d")) \
                .then_inc(sem("mixer_in"), 16)
            pool.dma_start(keep["rw_st"][0:DH].rearrange("v (d h k) -> v d h k", d=2, h=4),
                           a["state_rwkv"][0, 0].rearrange("d h v k -> v d h k")).then_inc(sem("mixer_in"), 16)
            pool.wait_ge(sem("zeroed"), 3)
            hg_blocks = keep["hg_st"].rearrange("p (a v) -> p a v", a=4)
            hg_source = a["state_hgrn"][0, 0].rearrange("d h k v -> (d h k) v").rearrange("(a p) v -> p a v", p=P)
            for q in range(2):
                rows = slice(DH * q, DH * q + DH)
                pool.dma_start(hg_blocks[rows, :, rows], hg_source[rows]).then_inc(sem("mixer_in"), 16)
            pool.dma_start(router_w[:, :, :], a["router_w"][0].rearrange("(c p) e -> p c e", p=P)).then_inc(sem("mixer_in"), 16)

            pool.wait_ge(sem("hg_state"), 1)
            pool.dma_start(a["new_state_hgrn"][0, 0].rearrange("d h k v -> (d h k) v").rearrange("(a p) v -> p a v", p=P),
                           hg_att["st"].rearrange("p (a v) -> p a v", a=4)).then_inc(sem("hg_out"), 16)
            pool.wait_ge(sem("rw_state"), 1)
            pool.dma_start(a["new_state_rwkv"][0, 0].rearrange("d h v k -> v (d h) k"),
                           rw["W"][0:DH, 0:512].rearrange("v (a k) -> v a k", a=8)).then_inc(sem("state_out"), 16)
            pool.wait_ge(sem("state_out"), 16)
            pool.wait_ge(sem("at_keys"), 1)
            pool.dma_start(a["new_att_k"][0, 0].rearrange("g t d -> t g d"),
                           at["qn"][:, 512:640].rearrange("t (g d) -> t g d", g=2)).then_inc(sem("cache_out"), 16)
            pool.dma_start(a["new_att_v"][0, 0].rearrange("g t d -> t g d"),
                           proj[:, 0, AV:AV + P].rearrange("t (g d) -> t g d", g=2)).then_inc(sem("cache_out"), 16)

            def biases(e):
                bg = a["moe_b_gu"][0, bass.ds(e, 1)] if not isinstance(e, int) else a["moe_b_gu"][0, e:e + 1]
                bd = a["moe_b_down"][0, bass.ds(e, 1)] if not isinstance(e, int) else a["moe_b_down"][0, e:e + 1]
                pool.dma_start(bias_row[:, 0:2 * FF], bg).then_inc(sem("bias_gu"), 16)
                pool.dma_start(bias_row[:, 2 * FF:3 * FF], bd).then_inc(sem("bias_down"), 16)

            pool.wait_ge(phase, 3 * (PH_ROUTE + 1))
            biases(0)
            with pool.Fori(1, NE) as e:
                pool.wait_ge(sem("bias_used"), e)
                biases(e)
            pool.wait_ge(sem("counted"), 1)
            need = pool.value_load(count_i[0:1, 0:1])
            with pool.If(need > CAP):
                with pool.Fori(1, NBATCH) as b:
                    with pool.Fori(0, NE) as e:
                        pool.wait_ge(sem("bias_used"), b * NE + e)
                        biases(e)

        @block.tensor
        def _(pe):
            ring_at = [0]

            def next_piece():
                i = ring_at[0]
                ring_at[0] += 1
                slot = FRONT_RING[i]
                pe.wait_ge(ring_full[slot], 16 * (FRONT_RING[:i].count(slot) + 1))
                return slot

            def release(*name, slots):
                pe.wait_ge(full[jobs[name] % 8], jobs[name] // 8 + 1)
                for slot in slots:
                    pe.nop().then_inc(ring_used[slot], 1)

            def modulation(g, js):
                b = open_bank(pe, "mod", g) if js[0] == 0 else bank[jobs[("mod", g)] % 8]
                for j in js:
                    s = next_piece()
                    for kc in range(2):
                        k = 2 * j + kc
                        for q in range(4):
                            mm = pe.matmul(b[32 * q:32 * q + 32, :], keep["c_silu"].rearrange("p (c m) -> p c m", m=32)[:, k],
                                           ring[:, s, kc * 2048 + q * 512:kc * 2048 + (q + 1) * 512],
                                           start=(k == 0), stop=(k == KC - 1), skip_group_check=True)
                    if j < 3:
                        mm.then_inc(ring_used[s], 1)
                if js[-1] == 3:
                    filled(mm, "mod", g)
                    release("mod", g, slots=[s])

            def transposes(name, sources):
                b = open_bank(pe, *name)
                at_col = 0
                for src in sources:
                    rows, cols = src.shape[0], 1
                    for n in src.shape[1:]:
                        cols *= n
                    last = pe.transpose(b[0:cols, at_col:at_col + rows], src, ident[0:rows, 0:rows])
                    at_col += rows
                filled(last, *name)

            pe.wait_ge(sem("const_in"), 16)
            pe.wait_ge(sem("c_silu"), 1)
            modulation(0, range(4))
            pe.wait_ge(sem("mod_sb"), 1)
            transposes(("modT",), [mod_sb[:, 0, P * c:P * (c + 1)] for c in range(4)])
            for s in range(2):
                pe.wait_ge(sem("x_norm"), s + 1)
                for half in range(2):
                    transposes(("xT", s, half), [h[:, s, P * c:P * (c + 1)] for c in range(4 * half, 4 * half + 4)])
            pe.wait_ge(sem("hT_prompt"), 8)
            pe.wait_ge(sem("hT_sample"), 8)
            for n, (lo, w) in enumerate(PIECES):
                slot = next_piece()
                wv = ring[:, slot, 0:KC * w].rearrange("p (c n) -> p c n", n=w)
                for s in range(2):
                    b = open_bank(pe, "proj", n, s)
                    for c in range(KC):
                        mm = pe.matmul(b[:, 0:w], hT[:, s, c, :], wv[:, c, :], start=(c == 0), stop=(c == KC - 1))
                    filled(mm, "proj", n, s)
                release("proj", n, 1, slots=[slot])
                if n < 4:
                    modulation(1 + n // 2, range(2 * (n % 2), 2 * (n % 2) + 2))
            end_phase(pe, PH_EARLY)

            loraT = rw["loraT"].rearrange("p (x t) -> p x t", x=3)
            sa = rw["sa"].rearrange("p (d x n) -> p d x n", d=2, x=2)
            TL = rw["TL"].rearrange("p (d x n) -> p d x n", d=2, x=4)
            T = hT_t[:, :].rearrange("p (d x a y t) -> p d x a y t", d=2, x=2, a=2, y=2)
            AR = (hT_t[:, :].rearrange("p (d x a y t) -> p x d a y t", d=2, x=2, a=2, y=2)[:, 0],
                  rw["sa"].rearrange("p (d a y t) -> p d a y t", d=2, a=2, y=2))
            LR = h_t[:, :].rearrange("p (d h y t) -> p d h y t", d=2, h=4, y=2)
            AKr = rw["AK"].rearrange("p (d h y t) -> p d h y t", d=2, h=4, y=2)
            X = rw["X"].rearrange("p (d h t) -> p d h t", d=2, h=4)
            Y = rw["Y"].rearrange("p (d h t) -> p d h t", d=2, h=4)
            W = rw["W"].rearrange("p (d h t) -> p d h t", d=2, h=4)
            Ru = rw["X"].rearrange("p (x d n) -> p x d n", x=2, d=2)
            s0 = keep["s0"].rearrange("p (a v) -> p a v", a=4)

            def rwkv_decay_inputs(s):
                pe.wait_ge(sem("rw_lora_act"), s + 1)
                transposes(("rw_loraT", s), [rw["th"][:, 0:P], proj[:, s, RAD:RAD + P], rw["th"][:, P:2 * P]])
                pe.wait_ge(sem("rw_loraT_sb"), s + 1)
                if s == 0:
                    pe.wait_ge(sem("mixer_in"), 16 * 9)
                    pe.wait_ge(sem("param_in"), 16 * 14)
                for d in range(2):
                    b = open_bank(pe, "rw_wa", s, d)
                    rows = slice(DH * d, DH * d + DH)
                    for x_, (bias, wt) in enumerate((("w0", "w2"), ("a0", "a2"))):
                        o = b[:, 256 * x_:256 * x_ + 256]
                        pe.matmul(o, ones[0:1, :], Pm(bias)[0:1, 256 * d:256 * d + 256], start=True, stop=False)
                        mm = pe.matmul(o, loraT[rows, x_, :], keep[wt][rows, :], start=False, stop=True)
                    filled(mm, "rw_wa", s, d)
                b = open_bank(pe, "rw_g", s)
                filled(pe.matmul(b[:, 0:256], loraT[:, 2, :], keep["g2"], start=True, stop=True), "rw_g", s)

            def rwkv_rows(s):
                pe.wait_ge(sem("rw_sa"), 2 * (s + 1))
                for d in range(2):
                    b = open_bank(pe, "rw_cum", s, d)
                    pe.matmul(b[:, 0:256], C(f"cent{d}"), sa[:, d, 0, :], start=True, stop=True)
                    filled(pe.matmul(b[:, 256:512], C(f"excl{d}"), sa[:, d, 0, :], start=True, stop=True), "rw_cum", s, d)
                b = open_bank(pe, "rw_half", s)
                for d in range(2):
                    for p in range(2):
                        k = 2 * (2 * d + p)
                        mm = pe.matmul(b[:, k:k + 2], sa[:, d, 0, P * p:P * p + P], C(f"halves{d}"), start=True, stop=True)
                filled(mm, "rw_half", s)
                if s:
                    st = keep["rw_st"][0:DH]
                    transposes(("rw_s0T", s), [st[:, P * k:P * k + P] for k in range(4)])
                pe.wait_ge(sem("rw_TL"), 4 * (s + 1))
                for d in range(2):
                    for x_, pair in enumerate(((1, 0), (3, 2))):
                        transposes(("rw_T", s, d, x_), [TL[:, d, y, P * p:P * p + P] for p in range(2) for y in pair])

            def rwkv_pairs(s):
                for d in range(2):
                    pe.wait_ge(sem("rw_T_act"), 2 * s + d + 1)
                    pe.wait_ge(sem("rw_T_dve"), 2 * s + d + 1)
                    for name, y in (("rw_b", 0), ("rw_k", 1), ("rw_L", 0)):
                        for q in range(2):
                            b = open_bank(pe, name, s, d, q)
                            for p in range(2):
                                if name == "rw_L":
                                    mm = pe.matmul(b[:, P * p:P * p + P], AR[q][:, d, p, 0, :], T[:, d, 1, p, 0, :],
                                                   start=True, stop=True)
                                else:
                                    mm = pe.matmul(b[:, 256 * p:256 * p + 256], T[:, d, 1, p, y, :],
                                                   AR[q][:, d, p, :, :], start=True, stop=True)
                            filled(mm, name, s, d, q)

            def rwkv_solve(s):
                for k in range(1, 7):
                    for d in range(2):
                        pe.wait_ge(sem("rw_XY"), 2 * (6 * s + k - 1) + d + 1)
                        b = open_bank(pe, "rw_W", s, k, d)
                        for n in range(4):
                            mm = pe.matmul(b[:, P * n:P * n + P], LR[:, d, n, 0, :], X[:, d, n, :], start=True, stop=True)
                        filled(mm, "rw_W", s, k, d)
                    for name in ("rw_X", "rw_Y"):
                        if (name, k) == ("rw_X", 6):
                            continue
                        for d in range(2):
                            pe.wait_ge(sem("rw_W_sb"), 2 * (6 * s + k - 1) + d + 1)
                            b = open_bank(pe, name, s, k, d)
                            for n in range(4):
                                o = b[:, P * n:P * n + P]
                                if name == "rw_X":
                                    mm = pe.matmul(o, Y[:, d, n, :], W[:, d, n, :], start=True, stop=True)
                                else:
                                    mm = pe.matmul(o, W[:, d, n, :], Y[:, d, n, :], start=True, stop=True)
                            filled(mm, name, s, k, d)
                v = proj[:, s, RV:RV + 256]
                if s:
                    pe.wait_ge(sem("rw_s0"), 2)
                for d in range(2):
                    b = open_bank(pe, "rw_R", s, d)
                    for n in range(4):
                        if s:
                            pe.matmul(b[:, DH * n:DH * n + DH], AR[n % 2][:, d, n // 2, 0, :],
                                      s0[:, 2 * d + n // 2, DH * (n % 2):DH * (n % 2) + DH],
                                      start=True, stop=False, skip_group_check=True)
                        mm = pe.matmul(b[:, DH * n:DH * n + DH], AKr[:, d, n, 0, :], v[:, DH * n:DH * n + DH],
                                       start=(s == 0), stop=True, skip_group_check=True)
                    filled(mm, "rw_R", s, d)
                for d in range(2):
                    pe.wait_ge(sem("rw_R_sb"), 2 * s + d + 1)
                    pe.wait_ge(sem("rw_Y_end"), 2 * s + d + 1)
                    b = open_bank(pe, "rw_u", s, d)
                    for n in range(4):
                        mm = pe.matmul(b[:, DH * n:DH * n + DH], Y[:, d, n, :], Ru[:, 0, d, DH * n:DH * n + DH],
                                       start=True, stop=True)
                    filled(mm, "rw_u", s, d)
                pe.wait_ge(sem("rw_u_sb"), 2 * (s + 1))
                b = open_bank(pe, "rw_y", s)
                for n in range(4):
                    o, cols = b[:, DH * n:DH * n + DH], slice(DH * n, DH * n + DH)
                    if s:
                        for d in range(2):
                            pe.matmul(o, AR[n % 2][:, d, n // 2, 1, :], s0[:, 2 * d + n // 2, DH * (n % 2):DH * (n % 2) + DH],
                                      start=(d == 0), stop=False, skip_group_check=True)
                    for d in range(2):
                        pe.matmul(o, LR[:, d, n, 1, :], Ru[:, 1, d, cols], start=(s == 0 and d == 0), stop=False,
                                  skip_group_check=True)
                        mm = pe.matmul(o, AKr[:, d, n, 1, :], v[:, cols], start=False, stop=(d == 1), skip_group_check=True)
                filled(mm, "rw_y", s)
                if s == 0:
                    b = open_bank(pe, "rw_st", s)
                    for d in range(2):
                        for n in range(4):
                            q, p, cols = n % 2, n // 2, slice(DH * n, DH * n + DH)
                            o = b[DH * q:DH * q + DH, DH * (2 * d + p):DH * (2 * d + p) + DH]
                            pe.matmul(o, TL[:, d, 3, cols], Ru[:, 1, d, cols], start=True, stop=False)
                            mm = pe.matmul(o, TL[:, d, 2, cols], v[:, cols], start=False, stop=True)
                    filled(mm, "rw_st", s)
                    pe.wait_ge(sem("rw_st_sb"), 1)
                    transposes(("rw_stT", s), [rw["W"][:, 512 + DH * k:512 + DH * k + DH] for k in range(4)])


            qT = hg["qT"].rearrange("p (a t) -> p a t", a=2)
            qL = hg["qL"].rearrange("p (d a l t) -> p d a l t", d=2, a=2, l=6)
            kL = hg["kL"].rearrange("p (d a l t) -> p d a l t", d=2, a=2, l=5)
            att = hg_att["att"].rearrange("p (d h t) -> p d h t", d=2, h=4)
            hst = keep["hg_st"].rearrange("p (a v) -> p a v", a=4)

            def hgrn_rows(s):
                pe.wait_ge(sem("hg_qk"), s + 1)
                transposes(("hg_T", s, 0), [hg["q"][:, P * p:P * p + P] for p in range(2)]
                           + [hg["kf"][:, P * p:P * p + P] for p in range(2)])
                transposes(("hg_T", s, 1), [hg["kf"][:, 256 + P * p:256 + P * p + P] for p in range(2)])
                pe.wait_ge(sem("hg_logf"), s + 1)
                for d in range(2):
                    for p in range(2):
                        lf = hg["logf"][:, 256 * d + P * p:256 * d + P * p + P]
                        for x_ in range(2):
                            b = open_bank(pe, "hg_E", s, d, p, x_)
                            w = 512 if x_ == 0 else 256
                            filled(pe.matmul(b[:, 0:w], lf, C(f"hg{d}")[:, 512 * x_:512 * x_ + w], start=True, stop=True),
                                   "hg_E", s, d, p, x_)

            def hgrn_pairs(s):
                for d in range(2):
                    pe.wait_ge(sem("hg_qL"), 4 * s + 2 * d + 2)
                    for q in range(2):
                        rows = slice(DH * q, DH * q + DH)
                        for lp in range(3):
                            b = open_bank(pe, "hg_att", s, d, q, lp)
                            for l in range(2 * lp, min(2 * lp + 2, 5)):
                                for p in range(2):
                                    o = b[:, 256 * (l % 2) + P * p:256 * (l % 2) + P * p + P]
                                    mm = pe.matmul(o, kL[rows, d, p, l, :], qL[rows, d, p, l, :], start=True, stop=True)
                            filled(mm, "hg_att", s, d, q, lp)

            def hgrn_out(s):
                v = proj[:, s, HI:HI + 256]
                pe.wait_ge(sem("hg_att"), s + 1)
                b = open_bank(pe, "hg_o", s)
                for n in range(4):
                    if s and n % 2 == 0:
                        for d in range(2):
                            pe.matmul(b[:, DH * n:DH * n + P], qL[:, d, n // 2, 5, :], hst[:, 2 * d + n // 2, :],
                                      start=(d == 0), stop=False, skip_group_check=True)
                    for d in range(2):
                        mm = pe.matmul(b[:, DH * n:DH * n + DH], att[:, d, n, :], v[:, DH * n:DH * n + DH],
                                       start=(s == 0 and d == 0), stop=(d == 1), skip_group_check=True)
                filled(mm, "hg_o", s)
                if s == 0:
                    b = open_bank(pe, "hg_after", s)
                    for d in range(2):
                        mm = pe.matmul(b[:, 256 * d:256 * d + 256], C(f"after{d}"), hg["logf"][:, 256 * d:256 * d + 256],
                                       start=True, stop=True)
                    filled(mm, "hg_after", s)
                    pe.wait_ge(sem("hg_kh"), 1)
                    b = open_bank(pe, "hg_st", s)
                    for d in range(2):
                        for n in range(4):
                            q, p = n % 2, n // 2
                            mm = pe.matmul(b[DH * q:DH * q + DH, DH * (2 * d + p):DH * (2 * d + p) + DH],
                                           hg_att["kh"][:, 256 * d + DH * n:256 * d + DH * n + DH],
                                           v[:, DH * n:DH * n + DH], start=True, stop=True)
                    filled(mm, "hg_st", s)

            for s in range(2):
                rwkv_decay_inputs(s)
                hgrn_rows(s)
                rwkv_rows(s)
                hgrn_pairs(s)
                rwkv_pairs(s)
                hgrn_out(s)
                rwkv_solve(s)
                end_phase(pe, PH_MIX + s)

            def spread(v):
                g, q0 = ((1, 0), (1, 2), (2, 0), (2, 2))[v]
                for s in range(2):
                    for half in range(2):
                        b = open_bank(pe, "bc", v, s, half)
                        k = P * (2 * (q0 + half) + s)
                        filled(pe.matmul(b[:, :], C("sel")[:, k:k + P], mod_sb[:, g, :], start=True, stop=True),
                               "bc", v, s, half)

            aqT = at["qT"].rearrange("p (i t) -> p i t", i=4)
            for s in range(2):
                nk, src = 1 + s, at["rope"] if s else at["qn"]
                pe.wait_ge(sem("at_qk"), s + 1)
                transposes(("at_qT", s), [src[:, P * i:P * i + P] for i in range(4)])
                transposes(("at_kT", s), ([keep["ck"]] if s else []) + [src[:, 512:640]])
                pe.wait_ge(sem("at_T_sb"), 2 * (s + 1))
                for i in range(2 * nk):
                    g, hs = i // nk, [4 // nk * (i % nk) + j for j in range(4 // nk)]
                    b = open_bank(pe, "at_S", s, i)
                    for j, hh in enumerate(hs):
                        mm = pe.matmul(b[:, P * nk * j:P * nk * (j + 1)], aqT[DH * g:DH * g + DH, hh, :],
                                       at["kT"][DH * g:DH * g + DH, 0:P * nk], start=True, stop=True)
                    filled(mm, "at_S", s, i)
                for vec in ((0,), (1, 2))[s]:
                    spread(vec)
                for i in range(2 * nk):
                    pe.wait_ge(sem("at_P"), (2 if s else 0) + i + 1)
                    transposes(("at_PT", s, i), [at["S"][:, 512 * i + P * j:512 * i + P * j + P] for j in range(4)])
                PT = at["PT"].rearrange("k (h b t) -> k h b t", h=8, b=2) if s else \
                    at["PT"][:, 0:1024].rearrange("k (h b t) -> k h b t", h=8, b=1)
                pe.wait_ge(sem("at_PT_sb"), (2 if s else 0) + 2 * nk)
                b = open_bank(pe, "at_o", s)
                for hh in range(8):
                    g = hh // 4
                    vals = ([keep["cv"]] if s else []) + [proj[:, s, AV:AV + P]]
                    for j, val in enumerate(vals):
                        mm = pe.matmul(b[:, DH * hh:DH * hh + DH], PT[:, hh, j, :], val[:, DH * g:DH * g + DH],
                                       start=(j == 0), stop=(j == nk - 1))
                filled(mm, "at_o", s)
                end_phase(pe, PH_AT + s)

            for s in range(2):
                for half in range(2):
                    transposes(("mixT", s, half), [mix[:, s, P * c:P * c + P] for c in range(4 * half, 4 * half + 4)])

            pe.wait_ge(sem("mixT_sb"), 4)
            slots = [next_piece(), next_piece()]
            for s in range(2):
                for half in range(2):
                    b = open_bank(pe, "out", s, half)
                    for c in range(KC):
                        wv = ring[:, slots[c // 4], :].rearrange("p (c n) -> p c n", n=D)
                        mm = pe.matmul(b[:, :], hT[:, s, c, :], wv[:, c % 4, 512 * half:512 * half + 512],
                                       start=(c == 0), stop=(c == KC - 1))
                    filled(mm, "out", s, half)
            release("out", 1, 1, slots=slots)
            end_phase(pe, PH_MID)
            spread(3)
            for s in range(2):
                pe.wait_ge(sem("h2"), s + 1)
                for half in range(2):
                    transposes(("h2T", s, half), [h[:, s, P * c:P * c + P] for c in range(4 * half, 4 * half + 4)])
            pe.wait_ge(sem("h2T_sb"), 4)
            b = open_bank(pe, "router")
            for s in range(2):
                for c in range(KC):
                    mm = pe.matmul(b[:, NE * s:NE * s + NE], hT[:, s, c, :], router_w[:, c, :],
                                   start=(c == 0), stop=(c == KC - 1))
            filled(mm, "router")
            pe.wait_ge(sem("chosen"), 1)
            b = open_bank(pe, "pos")
            before = C("tri0")[:, 0:P]
            pe.matmul(b[:, 0:NE], before, selm[:, 0, :], start=True, stop=True)
            pe.matmul(b[:, NE:2 * NE], ones, selm[:, 0, :], start=True, stop=False)
            pe.matmul(b[:, NE:2 * NE], before, selm[:, 1, :], start=False, stop=True)
            pe.matmul(b[:, 2 * NE:3 * NE], ones, selm[:, 0, :], start=True, stop=False)
            filled(pe.matmul(b[:, 2 * NE:3 * NE], ones, selm[:, 1, :], start=False, stop=True), "pos")
            end_phase(pe, PH_ROUTE)

            acc = bank[0:4]
            b_glu, b_lin, b_down, b_misc = bank[4:8]
            pe.wait_ge(sem("moe_init"), 1)
            for b in acc:
                pe.matmul(b[:, :], moe["zero"][:, 0:P], moe["zero"], start=True, stop=False, skip_group_check=True)

            def gather():
                for s in range(2):
                    for half in range(2):
                        mm = pe.matmul(b_misc[CAP * half:CAP * half + CAP, :], moe["hot"][:, CAP * s:CAP * s + CAP],
                                       h[:, s, 512 * half:512 * half + 512], start=(s == 0), stop=(s == 1),
                                       skip_group_check=True)
                mm.then_inc(sem("xe_full"), 1)

            def turn(out, src):
                for c in range(4):
                    mm = pe.transpose(out[:, P * c:P * c + P], src[:, P * c:P * c + P], ident)
                return mm

            def scatter():
                for half in range(2):
                    for s in range(2):
                        rows = slice(CAP * half, CAP * half + CAP)
                        mm = pe.matmul(acc[2 * s + half][:, :], moe["scat"][rows, P * s:P * s + P], moe["y"][rows, :],
                                       start=False, stop=False, skip_group_check=True)
                mm.then_inc(sem("scattered"), 1)

            def expert(n):
                xT = moe["xeT"].rearrange("p (c h m) -> p c h m", c=4, h=2)
                aT = moe["actT"].rearrange("p (c h m) -> p c h m", c=4, h=2)
                pe.wait_ge(sem("xeT_sb"), n + 1)
                for j in range(4):
                    pe.wait_ge(ring_full[j], 16 * (n + 1) + 16 * FRONT_ROUNDS[j])
                    for kc in range(2):
                        k = 2 * j + kc
                        for b, o in ((b_glu, 0), (b_lin, FF)):
                            for half in range(2):
                                mm = pe.matmul(b[CAP * half:CAP * half + CAP, :], xT[:, k % 4, k // 4, :],
                                               ring[:, j, 2048 * kc + o + 512 * half:2048 * kc + o + 512 * half + 512],
                                               start=(k == 0), stop=False, skip_group_check=True)
                    mm.then_inc(ring_used[j], 1)
                    if j == 0:
                        pe.wait_ge(sem("y_sb"), n + 1)
                        pe.wait_ge(sem("scat_sb"), n + 1)
                        scatter()
                pe.wait_ge(sem("bias_gu"), 16 * (n + 1))
                for b, o in ((b_glu, 0), (b_lin, FF)):
                    for half in range(2):
                        mm = pe.matmul(b[CAP * half:CAP * half + CAP, :], ones[0:1, 0:CAP],
                                       bias_row[:, o + 512 * half:o + 512 * half + 512],
                                       start=False, stop=True, skip_group_check=True)
                mm.then_inc(sem("gu_full"), 1)
                pe.wait_ge(sem("hot_ready"), n + 2)
                gather()
                pe.wait_ge(sem("act_ready"), n + 1)
                pe.wait_ge(sem("y_sb"), n + 1)
                turn(b_down, moe["act"]).then_inc(sem("actT_full"), 1)
                pe.wait_ge(sem("xe_sb"), n + 2)
                turn(b_misc, moe["xe"]).then_inc(sem("xeT_full"), 1)
                pe.wait_ge(sem("actT_sb"), n + 1)
                for j in range(2):
                    pe.wait_ge(ring_full[4 + j], 16 * (n + 1) + 16 * FRONT_ROUNDS[4 + j])
                    for kc in range(4):
                        k = 4 * j + kc
                        for half in range(2):
                            mm = pe.matmul(b_down[CAP * half:CAP * half + CAP, :], aT[:, k % 4, k // 4, :],
                                           ring[:, 4 + j, D * kc + 512 * half:D * kc + 512 * half + 512],
                                           start=(k == 0), stop=False, skip_group_check=True)
                    mm.then_inc(ring_used[4 + j], 1)
                    if j == 0:
                        pe.wait_ge(sem("xeT_sb"), n + 2)
                        pe.wait_ge(sem("hotg_ready"), n + 1)
                        for s in range(2):
                            mm = pe.transpose(b_misc[:, P * s:P * s + P], moe["hotg"][:, P * s:P * s + P], ident)
                        mm.then_inc(sem("scat_full"), 1)
                pe.wait_ge(sem("bias_down"), 16 * (n + 1))
                for half in range(2):
                    mm = pe.matmul(b_down[CAP * half:CAP * half + CAP, :], ones[0:1, 0:CAP],
                                   bias_row[:, 2 * FF + 512 * half:2 * FF + 512 * half + 512],
                                   start=False, stop=True, skip_group_check=True)
                mm.then_inc(sem("down_full"), 1)
                pe.wait_ge(sem("down_full"), n + 1)
                pe.nop().then_inc(sem("bias_used"), 1)

            pe.wait_ge(sem("hot_ready"), 1)
            gather()
            pe.wait_ge(sem("xe_sb"), 1)
            turn(b_misc, moe["xe"]).then_inc(sem("xeT_full"), 1)
            with pe.Fori(0, NE) as e:
                expert(e)
            need = pe.value_load(count_i[0:1, 0:1])
            with pe.If(need > CAP):
                with pe.Fori(1, NBATCH) as bt:
                    with pe.Fori(0, NE) as e:
                        expert(bt * NE + e)
            pe.wait_ge(sem("last_y"), 2)
            for half in range(2):
                for s in range(2):
                    rows = slice(CAP * half, CAP * half + CAP)
                    mm = pe.matmul(acc[2 * s + half][:, :], moe["scat"][rows, P * s:P * s + P], moe["y"][rows, :],
                                   start=False, stop=True, skip_group_check=True)
            mm.then_inc(sem("acc_full"), 1)

        @block.scalar
        def _(act):
            A = act.activation
            powers = [0]

            def inverse_root(t):
                powers[0] += 1
                act.wait_ge(sem("pow_in"), powers[0])
                A(t, t, ACT.Ln).then_inc(sem("pow_ln"), 1)
                act.wait_ge(sem("pow_ln"), powers[0])
                A(t, t, ACT.Exp, scale=-0.5).then_inc(sem("pow_out"), 1)

            head_rs = sel_e["m8"][:, 4:8]
            act.wait_ge(sem("zeroed"), 2)
            cv = early["c"].rearrange("p (c m) -> p c m", m=32)
            act.dma_start(cv[:, :, 0], a["c_ctx"].rearrange("(c p) -> p c", p=P), allow_slow_non_contiguous=True).then_inc(sem("c_in"), 16)
            act.dma_start(cv[:, :, 1], a["c"][0].rearrange("(c p) -> p c", p=P), allow_slow_non_contiguous=True).then_inc(sem("c_in"), 16)
            act.wait_ge(sem("c_in"), 32)
            A(early["csig"], early["c"], ACT.Sigmoid).then_inc(sem("c_sig"), 1)
            act.wait_ge(sem("x_in"), 32)
            for s in range(2):
                if s:
                    act.wait_ge(sem("x_sq"), 1)
                A(early["sq"], x[:, s, :], ACT.Square, accum_out=sel_e["a"][:, s:s + 1]).then_inc(sem("x_sq"), 1)
            inverse_root(sel_e["a"][:, 2:4])
            b = take(act, "modT")
            done(A(early["modT"], b[:, :], ACT.Copy), "modT")
            act.wait_ge(sem("s1_ready"), 2)
            mT = early["modT"].rearrange("p (c q m) -> p c q m", c=4, q=4)
            s1 = early["s1"].rearrange("p (s c) -> p s c", s=2)
            for half in range(2):
                b = take(act, "xT", 0, half)
                for c in range(4):
                    ins = A(hT[:, 0, 4 * half + c, :], b[:, P * c:P * c + P], ACT.Identity,
                            bias=mT[:, c, half, 0:1], scale=s1[:, 0, 4 * half + c:4 * half + c + 1])
                    ins.then_inc(sem("hT_prompt"), 1)
                act.wait_ge(sem("hT_prompt"), 4 * half + 4)
                done(act.nop(), "xT", 0, half)
            for n, (lo, w) in enumerate(PIECES):
                b = take(act, "proj", n, 0)
                done(A(proj[:, 0, lo:lo + w], b[:, 0:w], ACT.Copy), "proj", n, 0)
            end_phase(act, PH_EARLY)

            T = hT_t[:, :].rearrange("p (d x n) -> p d x n", d=2, x=2)
            TL = rw["TL"].rearrange("p (d x n) -> p d x n", d=2, x=4)
            Ru = rw["X"].rearrange("p (x d n) -> p x d n", x=2, d=2)

            def rwkv_decay_inputs(s):
                A(rw["th"][:, 0:P], proj[:, s, RWD:RWD + P], ACT.Tanh)
                A(rw["th"][:, P:2 * P], proj[:, s, RGD:RGD + P], ACT.Sigmoid).then_inc(sem("rw_lora_act"), 1)
                inverse_root(head_rs)
                b = take(act, "rw_loraT", s)
                A(rw["loraT"], b[:, 0:384], ACT.Copy).then_inc(sem("rw_loraT_sb"), 1)
                act.wait_ge(sem("rw_loraT_sb"), s + 1)
                done(act.nop(), "rw_loraT", s)
                for d in range(2):
                    b = take(act, "rw_wa", s, d)
                    A(rw["sa"][:, 512 * d:512 * d + 512], b[:, :], ACT.Sigmoid).then_inc(sem("rw_sa"), 1)
                act.wait_ge(sem("rw_sa"), 2 * (s + 1))
                for d in range(2):
                    done(act.nop(), "rw_wa", s, d)
                b = take(act, "rw_g", s)
                done(A(rw["g"], b[:, 0:256], ACT.Copy), "rw_g", s)

            def rwkv_rows(s):
                for d in range(2):
                    b = take(act, "rw_cum", s, d)
                    A(TL[:, d, 0:2, :], b[:, :], ACT.Exp, scale=-DECAY)
                    A(TL[:, d, 2, :], b[:, 0:256], ACT.Exp, scale=DECAY).then_inc(sem("rw_E"), 1)
                act.wait_ge(sem("rw_E"), 2 * (s + 1))
                for d in range(2):
                    done(act.nop(), "rw_cum", s, d)
                b = take(act, "rw_half", s)
                A(sel_e["d"][:, 8 * s:8 * s + 8], b[:, 0:8], ACT.Exp, scale=-DECAY).then_inc(sem("rw_half_sb"), 1)
                act.wait_ge(sem("rw_half_sb"), s + 1)
                done(act.nop(), "rw_half", s)
                for d in range(2):
                    b = take(act, "rw_T", s, d, 0)
                    if d == 0:
                        act.wait_ge(sem("rw_a_zero"), s + 1)
                    A(T[0:DH, d, 0, :], b[0:DH, :], ACT.Copy)
                    A(rw["sa"][DH:P, 512 * d:512 * d + 512], b[DH:P, :], ACT.Copy).then_inc(sem("rw_T_act"), 1)
                act.wait_ge(sem("rw_T_act"), 2 * (s + 1))
                for d in range(2):
                    done(act.nop(), "rw_T", s, d, 0)

            def rwkv_solve(s):
                for x_, (job, name) in enumerate((("rw_R", "rw_R_sb"), ("rw_u", "rw_u_sb"))):
                    for d in range(2):
                        b = take(act, job, s, d)
                        A(Ru[:, x_, d, :], b[:, 0:256], ACT.Copy).then_inc(sem(name), 1)
                    act.wait_ge(sem(name), 2 * (s + 1))
                    for d in range(2):
                        done(act.nop(), job, s, d)
                inverse_root(head_rs)
                if s == 0:
                    b = take(act, "rw_st", s)
                    for k in range(4):
                        A(rw["W"][:, 512 + DH * k:512 + DH * k + DH], b[:, DH * k:DH * k + DH], ACT.Copy,
                          scale=sel_e["d"][:, 2 * k + 1:2 * k + 2]).then_inc(sem("rw_st_part"), 1)
                    act.wait_ge(sem("rw_st_part"), 4)
                    act.nop().then_inc(sem("rw_st_sb"), 1)
                    done(act.nop(), "rw_st", s)
                    b = take(act, "rw_stT", s)
                    A(rw["W"][0:DH, 0:512], b[0:DH, 0:512], ACT.Copy).then_inc(sem("rw_state"), 1)
                    act.wait_ge(sem("rw_state"), 1)
                    done(act.nop(), "rw_stT", s)
                    act.wait_ge(sem("state_out"), 16)

            def hgrn_rows(s):
                if s == 0:
                    act.wait_ge(sem("lb_shift"), 1)
                    A(hg["kf"], hg["kf"], ACT.Exp).then_inc(sem("lb_exp"), 1)
                A(hg["q"], proj[:, s, HQ:HQ + 256], ACT.Sigmoid)
                A(hg["fs"], proj[:, s, HF:HF + 512], ACT.Sigmoid)
                A(hg["gg"], proj[:, s, HG:HG + 256], ACT.Sigmoid).then_inc(sem("hg_sig"), 1)
                act.wait_ge(sem("hg_f"), s + 1)
                A(hg["logf"], hg["fs"], ACT.Ln).then_inc(sem("hg_logf"), 1)
                for x_ in range(2):
                    b = take(act, "hg_T", s, x_)
                    if x_ == 0:
                        A(hg["qT"], b[:, 0:256], ACT.Copy)
                        done(A(hg["kT"][:, 0:256], b[:, 256:512], ACT.Copy), "hg_T", s, x_)
                    else:
                        done(A(hg["kT"][:, 256:512], b[:, 0:256], ACT.Copy), "hg_T", s, x_)
                E = hg_E.rearrange("p (b n) -> p b n", b=2)
                for k in range(4):
                    d, p = k // 2, k % 2
                    if 4 * s + k >= 2:
                        act.wait_ge(sem("hg_qL"), 4 * s + k - 1)
                    b = take(act, "hg_E", s, d, p, 0)
                    done(A(E[:, k % 2, 0:512], b[:, :], ACT.Exp), "hg_E", s, d, p, 0)
                    b = take(act, "hg_E", s, d, p, 1)
                    A(E[:, k % 2, 768:896], b[:, 0:P], ACT.Exp, scale=-1.0)
                    A(E[:, k % 2, 512:768], b[:, 0:256], ACT.Exp).then_inc(sem("hg_E_sb"), 1)
                    act.wait_ge(sem("hg_E_sb"), 4 * s + k + 1)
                    done(act.nop(), "hg_E", s, d, p, 1)

            def hgrn_out(s):
                if s == 0:
                    b = take(act, "hg_after", s)
                    A(hg_att["kh"], b[:, :], ACT.Exp).then_inc(sem("hg_after_sb"), 1)
                    act.wait_ge(sem("hg_after_sb"), 1)
                    done(act.nop(), "hg_after", s)
                    b = take(act, "hg_st", s)
                    A(hg_att["st"], b[:, 0:256], ACT.Copy).then_inc(sem("hg_state"), 1)
                    act.wait_ge(sem("hg_state"), 1)
                    done(act.nop(), "hg_st", s)
                inverse_root(head_rs)

            for s in range(2):
                rwkv_decay_inputs(s)
                hgrn_rows(s)
                rwkv_rows(s)
                hgrn_out(s)
                rwkv_solve(s)
                end_phase(act, PH_MIX + s)

            def spread(v):
                for t in range(2):
                    for half in range(2):
                        b = take(act, "bc", v, t, half)
                        done(A((gate1, shift2, scale2, gate2)[v][:, t, 512 * half:512 * half + 512], b[:, :], ACT.Copy),
                             "bc", v, t, half)

            for s in range(2):
                nk = 1 + s
                inverse_root(sel_e["c"][:, 0:10])
                b = take(act, "at_qT", s)
                A(at["qT"], b[:, :], ACT.Copy).then_inc(sem("at_T_sb"), 1)
                b = take(act, "at_kT", s)
                A(at["kT"][:, 0:P * nk], b[:, 0:P * nk], ACT.Copy).then_inc(sem("at_T_sb"), 1)
                act.wait_ge(sem("at_T_sb"), 2 * (s + 1))
                done(act.nop(), "at_qT", s)
                done(act.nop(), "at_kT", s)
                for i in range(2 * nk):
                    act.wait_ge(sem("at_shift"), (2 if s else 0) + i + 1)
                    Si = at["S"][:, 512 * i:512 * i + 512]
                    A(Si, Si, ACT.Exp, scale=1.0 / math.sqrt(DH)).then_inc(sem("at_P"), 1)
                for vec in ((0,), (1, 2))[s]:
                    spread(vec)
                for i in range(2 * nk):
                    b = take(act, "at_PT", s, i)
                    A(at["PT"][:, 512 * i:512 * i + 512], b[:, :], ACT.Copy).then_inc(sem("at_PT_sb"), 1)
                act.wait_ge(sem("at_PT_sb"), (2 if s else 0) + 2 * nk)
                for i in range(2 * nk):
                    done(act.nop(), "at_PT", s, i)
                end_phase(act, PH_AT + s)

            act.wait_ge(sem("cache_out"), 32)
            for s in range(2):
                for half in range(2):
                    b = take(act, "mixT", s, half)
                    A(hT[:, s, 4 * half:4 * half + 4, :], b[:, :], ACT.Copy).then_inc(sem("mixT_sb"), 1)
            act.wait_ge(sem("mixT_sb"), 4)
            for s in range(2):
                for half in range(2):
                    done(act.nop(), "mixT", s, half)
            end_phase(act, PH_MID)
            for s in range(2):
                act.wait_ge(sem("x2"), s + 1)
                if s:
                    act.wait_ge(sem("x2_sq"), 1)
                A(gate1[:, 0, :], x[:, s, :], ACT.Square, accum_out=sel_e["b"][:, s:s + 1]) \
                    .then_inc(sem("x2_sq"), 1)
            inverse_root(sel_e["b"][:, 2:4])
            spread(3)
            for s in range(2):
                for half in range(2):
                    b = take(act, "h2T", s, half)
                    A(hT[:, s, 4 * half:4 * half + 4, :], b[:, :], ACT.Copy).then_inc(sem("h2T_sb"), 1)
            act.wait_ge(sem("h2T_sb"), 4)
            for s in range(2):
                for half in range(2):
                    done(act.nop(), "h2T", s, half)
            act.wait_ge(sem("shifted"), 1)
            A(sel_e["e4"], sel_e["e4"], ACT.Exp).then_inc(sem("exp4"), 1)
            end_phase(act, PH_ROUTE)

            def gathered(n):
                act.wait_ge(sem("xe_full"), n)
                A(moe["xe"], bank[7][:, :], ACT.Copy).then_inc(sem("xe_sb"), 1)

            def turned(n):
                act.wait_ge(sem("xeT_full"), n)
                A(moe["xeT"], bank[7][:, :], ACT.Copy).then_inc(sem("xeT_sb"), 1)

            def expert(n):
                act.wait_ge(sem("glu_sb"), n + 1)
                A(moe["sig"], moe["glu"], ACT.Sigmoid, scale=ALPHA).then_inc(sem("sig_sb"), 1)
                gathered(n + 2)
                turned(n + 2)
                act.wait_ge(sem("scat_full"), n + 1)
                act.wait_ge(sem("scattered"), n + 1)
                A(moe["scat"], bank[7][:, 0:2 * P], ACT.Copy).then_inc(sem("scat_sb"), 1)

            gathered(1)
            turned(1)
            with act.Fori(0, NE) as e:
                expert(e)
            need = act.value_load(count_i[0:1, 0:1])
            with act.If(need > CAP):
                with act.Fori(1, NBATCH) as bt:
                    with act.Fori(0, NE) as e:
                        expert(bt * NE + e)
            act.drain().then_inc(sem("last_y"), 1)
            for s in range(2):
                act.wait_ge(sem("x3"), s + 1)
                if s:
                    act.wait_ge(sem("x3_sq"), 1)
                A(hT_t[:, 0:D], x[:, s, :], ACT.Square, accum_out=sel_e["c"][:, s:s + 1]).then_inc(sem("x3_sq"), 1)
            inverse_root(sel_e["c"][:, 2:4])

        @block.vector
        def _(dve):
            tt, ts, stt = dve.tensor_tensor, dve.tensor_scalar, dve.scalar_tensor_tensor
            step = Steps(dve, "dve_step")

            step(dve.memset(mod_sb[:, :, :], 0.0))
            dve.nop().then_inc(sem("zeroed"), 1)
            step(dve.memset(early["c"], 0.0))
            dve.nop().then_inc(sem("zeroed"), 1)
            dve.memset(keep["s0"], 0.0)
            step(dve.memset(keep["hg_st"], 0.0))
            dve.nop().then_inc(sem("zeroed"), 1)
            dve.wait_ge(sem("c_in"), 32)
            dve.wait_ge(sem("c_sig"), 1)
            tt(keep["c_silu"], early["c"], early["csig"], ALU.mult).then_inc(sem("c_silu"), 1)

            powers = [0]

            def rstd(out, ss, scale, eps):
                ts(out, ss, scale, eps, ALU.mult, ALU.add).then_inc(sem("pow_in"), 1)
                powers[0] += 1
                dve.wait_ge(sem("pow_out"), powers[0])

            dve.wait_ge(sem("x_sq"), 2)
            rstd(sel_e["a"][:, 2:4], sel_e["a"][:, 0:2], 1.0 / D, EPS)
            for s in range(2):
                ts(h[:, s, :], x[:, s, :], sel_e["a"][:, 2 + s:3 + s], None, ALU.mult).then_inc(sem("x_norm"), 1)
            dve.wait_ge(sem("bmod_in"), 32)
            b = take(dve, "mod", 0)
            tt(mod_sb[:, 0, :], b[:, :], mod_sb[:, 0, :], ALU.add).then_inc(sem("mod_sb"), 1)
            dve.wait_ge(sem("mod_sb"), 1)
            done(dve.nop(), "mod", 0)
            dve.wait_ge(sem("gcol_in"), 16)
            dve.wait_ge(free[jobs[("modT",)] % 8], jobs[("modT",)] // 8 + 1)
            mT = early["modT"].rearrange("p (c q m) -> p q c m", c=4, q=4)
            s1 = early["s1"].rearrange("p (s c) -> p s c", s=2)
            g_col = early["g_col"].rearrange("p (q c) -> p q c", q=2)
            for s in range(2):
                stt(out=s1[:, s, :].rearrange("p (q c) -> p q c", q=2), in0=mT[:, 2:4, :, s], scalar=1.0, in1=g_col,
                    op0=ALU.add, op1=ALU.mult).then_inc(sem("s1_ready"), 1)
            dve.wait_ge(sem("s1_ready"), 2)
            for half in range(2):
                b = take(dve, "xT", 1, half)
                for c in range(4):
                    ts(hT[:, 1, 4 * half + c, :], b[:, P * c:P * c + P], s1[:, 1, 4 * half + c:4 * half + c + 1],
                       mT[:, half, c, 1:2], ALU.mult, ALU.add).then_inc(sem("hT_sample"), 1)
                dve.wait_ge(sem("hT_sample"), 4 * half + 4)
                done(dve.nop(), "xT", 1, half)
            for n, (lo, w) in enumerate(PIECES):
                b = take(dve, "proj", n, 1)
                done(dve.tensor_copy(proj[:, 1, lo:lo + w], b[:, 0:w]), "proj", n, 1)
                if n in (1, 3):
                    g = 1 + n // 2
                    b = take(dve, "mod", g)
                    done(tt(mod_sb[:, g, :], b[:, :], mod_sb[:, g, :], ALU.add), "mod", g)
            end_phase(dve, PH_EARLY)

            TL = rw["TL"].rearrange("p (d x n) -> p d x n", d=2, x=4)
            T = hT_t[:, :].rearrange("p (d x n) -> p d x n", d=2, x=2)
            LR = h_t[:, :].rearrange("p (d h y) -> p d h y", d=2, h=4)
            AKr = rw["AK"].rearrange("p (d h y) -> p d h y", d=2, h=4)
            X = rw["X"].rearrange("p (d h t) -> p d h t", d=2, h=4)
            Y = rw["Y"].rearrange("p (d h t) -> p d h t", d=2, h=4)
            W = rw["W"].rearrange("p (d h t) -> p d h t", d=2, h=4)
            kd = rw["X"][:, 0:512].rearrange("p (d n) -> p d n", d=2)
            kb = rw["X"][:, 512:1024].rearrange("p (d n) -> p d n", d=2)
            t0 = rw["W"][:, 0:512].rearrange("p (d n) -> p d n", d=2)
            t1, t2 = rw["W"][:, 512:768], rw["W"][:, 768:1024]
            sa = rw["sa"].rearrange("p (d x n) -> p d x n", d=2, x=2)
            a_raw = sa[:, :, 1, :]
            two = [P, 2, 256]
            small8 = sel_e["m8"]

            def by_head(ap, n=4):
                return ap.rearrange("p (h d) -> p h d", h=n)

            dve.wait_ge(sem("param_in"), 16 * 14)

            def rwkv_keys(s):
                k = proj[:, s, RK:RK + 256]
                dve.memset(h_t[:, :], 0.0)
                dve.memset(T[DH:P, :, 0, :], 0.0)
                step(dve.memset(rw["AK"], 0.0))
                step(tt(rw["kk"], k, Pm("kk"), ALU.mult))
                step(tt(t1, rw["kk"], rw["kk"], ALU.mult))
                step(dve.tensor_reduce(small8[:, 0:4], by_head(t1), AX.X, ALU.add))
                rstd(small8[:, 4:8], small8[:, 0:4], 1.0, 1e-12)
                step(tt(by_head(rw["kk"]), by_head(rw["kk"]), bc(small8[:, 4:8], [P, 4, DH], 2), ALU.mult))

            def rwkv_rows(s):
                r, k = (proj[:, s, o:o + 256] for o in (RR, RK))
                dve.wait_ge(sem("rw_sa"), 2 * (s + 1))
                tt(kb, a_raw, bc(rw["kk"], two, 1), ALU.mult)
                step(stt(out=t0, in0=a_raw, scalar=-1.0, in1=bc(Pm("ka"), two, 1), op0=ALU.add, op1=ALU.mult))
                step(stt(out=kd, in0=t0, scalar=1.0, in1=bc(k, two, 1), op0=ALU.add, op1=ALU.mult))
                step(tt(t1, kd[:, 0, :], kd[:, 1, :], ALU.add))
                step(tt(t1, t1, r, ALU.mult))
                step(tt(t1, t1, Pm("rk"), ALU.mult))
                step(dve.tensor_reduce(small8[:, 8:12], by_head(t1), AX.X, ALU.add))
                dve.wait_ge(sem("rw_E"), 2 * (s + 1))
                tt(TL[:, :, 3, :], TL[:, :, 2, :], kb, ALU.mult).then_inc(sem("rw_TL"), 1)
                dve.wait_ge(sem("rw_TL"), 4 * s + 1)
                tt(TL[:, :, 2, :], TL[:, :, 2, :], kd, ALU.mult).then_inc(sem("rw_TL"), 1)
                stt(out=TL[:, :, 1, :], in0=TL[:, :, 1, :], scalar=-1.0, in1=bc(rw["kk"], two, 1),
                    op0=ALU.mult, op1=ALU.mult).then_inc(sem("rw_TL"), 1)
                tt(TL[:, :, 0, :], TL[:, :, 0, :], bc(r, two, 1), ALU.mult).then_inc(sem("rw_TL"), 1)
                if s:
                    b = take(dve, "rw_s0T", s)
                    dve.wait_ge(sem("rw_half_sb"), s + 1)
                    hs = sel_e["d"][:, 8:16].rearrange("p (a x) -> p a x", x=2)[:, :, 0]
                    s0 = keep["s0"].rearrange("p (a v) -> p a v", a=4)
                    for q in range(2):
                        rows = slice(DH * q, DH * q + DH)
                        tt(s0[rows, :, rows], b[rows, 0:256].rearrange("p (a v) -> p a v", a=4),
                           bc(hs[rows], [DH, 4, DH], 2), ALU.mult).then_inc(sem("rw_s0"), 1)
                    dve.wait_ge(sem("rw_s0"), 2)
                    done(dve.nop(), "rw_s0T", s)
                take(dve, "rw_T", s, 0, 0)
                dve.memset(rw["sa"][0:DH, :], 0.0).then_inc(sem("rw_a_zero"), 1)
                for d in range(2):
                    b = take(dve, "rw_T", s, d, 1)
                    dve.tensor_copy(T[:, d, 1, :], b[:, :]).then_inc(sem("rw_T_dve"), 1)
                dve.wait_ge(sem("rw_T_dve"), 2 * (s + 1))
                for d in range(2):
                    done(dve.nop(), "rw_T", s, d, 1)

            def rwkv_pairs(s):
                for d in range(2):
                    mask = bc(C(f"tri{d}").bitcast(I32), [P, 2, 256], 1)
                    for name, dst in (("rw_b", LR), ("rw_k", AKr)):
                        for q in range(2):
                            b = take(dve, name, s, d, q)
                            done(dve.copy_predicated(dst[:, d, q::2, :], mask, b[:, :].rearrange("p (a y) -> p a y", a=2)),
                                 name, s, d, q)
                    m0, m1 = C(f"merge{d}")[:, 0:P], C(f"merge{1 - d}")[:, 0:P]
                    for q in range(2):
                        b = take(dve, "rw_L", s, d, q)
                        done(tt(X[:, d, q::2, :], b[:, 0:256].rearrange("p (a t) -> p a t", a=2),
                                bc(m1, [P, 2, P], 1), ALU.mult), "rw_L", s, d, q)
                    dve.wait_ge(free[jobs[("rw_L", s, d, 1)] % 8], jobs[("rw_L", s, d, 1)] // 8 + 1)
                    step(tt(Y[:, d], LR[:, d, :, 0:P], bc(m0, [P, 4, P], 1), ALU.mult))
                    tt(X[:, d], X[:, d], bc(ident, [P, 4, P], 1), ALU.add)
                    tt(Y[:, d], Y[:, d], bc(ident, [P, 4, P], 1), ALU.add).then_inc(sem("rw_XY"), 1)

            def rwkv_solve(s):
                v = proj[:, s, RV:RV + 256]
                for lv in range(1, 7):
                    for d in range(2):
                        m1 = C(f"merge{1 - d}")[:, P * lv:P * lv + P]
                        b = take(dve, "rw_W", s, lv, d)
                        tt(W[:, d], b[:, :].rearrange("p (h t) -> p h t", h=4), bc(m1, [P, 4, P], 1), ALU.mult) \
                            .then_inc(sem("rw_W_sb"), 1)
                        dve.wait_ge(sem("rw_W_sb"), 2 * (6 * s + lv - 1) + d + 1)
                        done(dve.nop(), "rw_W", s, lv, d)
                    dve.wait_ge(sem("rw_XY"), 2 * (6 * s + lv))
                    if lv < 6:
                        for d in range(2):
                            b = take(dve, "rw_X", s, lv, d)
                            done(tt(X[:, d], X[:, d], b[:, :].rearrange("p (h t) -> p h t", h=4), ALU.add),
                                 "rw_X", s, lv, d)
                    for d in range(2):
                        b = take(dve, "rw_Y", s, lv, d)
                        ins = tt(Y[:, d], Y[:, d], b[:, :].rearrange("p (h t) -> p h t", h=4), ALU.add)
                        done(ins, "rw_Y", s, lv, d)
                        k_ = jobs[("rw_Y", s, lv, d)]
                        dve.wait_ge(free[k_ % 8], k_ // 8 + 1)
                        dve.nop().then_inc(sem("rw_XY" if lv < 6 else "rw_Y_end"), 1)
                b = take(dve, "rw_y", s)
                yv, o = b[:, 0:256], mix[:, s, 512:768]
                step(dve.tensor_reduce(small8[:, 0:4], by_head(yv), AX.X, ALU.add))
                step(ts(small8[:, 0:4], small8[:, 0:4], 1.0 / DH, None, ALU.mult))
                step(tt(by_head(o), by_head(yv), bc(small8[:, 0:4], [P, 4, DH], 2), ALU.subtract))
                done(dve.nop(), "rw_y", s)
                tmp = rw["kk"]
                step(tt(tmp, o, o, ALU.mult))
                step(dve.tensor_reduce(small8[:, 0:4], by_head(tmp), AX.X, ALU.add))
                rstd(small8[:, 4:8], small8[:, 0:4], 1.0 / DH, GN_EPS)
                step(tt(by_head(o), by_head(o), bc(small8[:, 4:8], [P, 4, DH], 2), ALU.mult))
                step(tt(o, o, Pm("gn_g"), ALU.mult))
                step(tt(by_head(tmp), by_head(v), bc(small8[:, 8:12], [P, 4, DH], 2), ALU.mult))
                step(tt(o, o, Pm("gn_b"), ALU.add))
                step(tt(o, o, tmp, ALU.add))
                step(tt(o, o, rw["g"], ALU.mult))

            qT = hg["qT"].rearrange("p (a t) -> p a t", a=2)
            kT = hg["kT"].rearrange("p (d a t) -> p d a t", d=2, a=2)
            qL = hg["qL"].rearrange("p (d a l t) -> p d a l t", d=2, a=2, l=6)
            kL = hg["kL"].rearrange("p (d a l t) -> p d a l t", d=2, a=2, l=5)
            att = hg_att["att"].rearrange("p (d h t) -> p d h t", d=2, h=4)
            E = hg_E.rearrange("p (b l t) -> p b l t", b=2, l=7)
            lbt = Pm("lb")
            lb_w = hg["kf"]

            def hgrn_rows(s):
                if s == 0:
                    step(tt(lb_w, lbt, lbt, ALU.subtract))
                    dve.nop().then_inc(sem("lb_shift"), 1)
                    dve.wait_ge(sem("lb_exp"), 1)
                    step(dve.reciprocal(hg["logf"], lb_w))
                    step(tt(lb_w, lb_w, hg["logf"], ALU.mult))
                    step(tt(lbt, lb_w, lb_w, ALU.subtract))
                step(dve.memset(hg_att["att"], 0.0))
                dve.wait_ge(sem("hg_sig"), s + 1)
                tt(hg["q"], hg["q"], proj[:, s, HQ:HQ + 256], ALU.mult)
                step(ts(hg["kf"], lbt, -1.0, 1.0, ALU.mult, ALU.add))
                step(tt(hg["fs"], hg["fs"], hg["kf"], ALU.mult))
                step(tt(hg["fs"], hg["fs"], lbt, ALU.add))
                step(ts(hg["kf"], hg["fs"], -1.0, 1.0, ALU.mult, ALU.add))
                dve.nop().then_inc(sem("hg_qk"), 1)
                ts(hg["fs"], hg["fs"], 1e-6, None, ALU.max).then_inc(sem("hg_f"), 1)
                dve.wait_ge(free[jobs[("hg_T", s, 0)] % 8], jobs[("hg_T", s, 0)] // 8 + 1)
                dve.wait_ge(free[jobs[("hg_T", s, 1)] % 8], jobs[("hg_T", s, 1)] // 8 + 1)
                for i in range(4):
                    d, p = i // 2, i % 2
                    dve.wait_ge(sem("hg_E_sb"), 4 * s + i + 1)
                    Ei = E[:, i % 2]
                    tt(qL[:, d, p], Ei[:, 0:6], bc(qT[:, p], [P, 6, P], 1), ALU.mult)
                    tt(kL[:, d, p, 4, :], Ei[:, 6, :], kT[:, d, p], ALU.mult)
                    tt(kL[:, d, p, 0:4, :], Ei[:, 0:4], bc(kT[:, d, p], [P, 4, P], 1), ALU.mult).then_inc(sem("hg_qL"), 1)

            def hgrn_pairs(s):
                for d in range(2):
                    for q in range(2):
                        for lp in range(3):
                            b = take(dve, "hg_att", s, d, q, lp)
                            for l in range(2 * lp, min(2 * lp + 2, 5)):
                                m = C(f"merge{d}")[:, P * (6 - l):P * (7 - l)] if l < 4 else C(f"diag{d}")
                                ins = dve.copy_predicated(att[:, d, q::2, :], bc(m.bitcast(I32), [P, 2, P], 1),
                                                          b[:, 256 * (l % 2):256 * (l % 2) + 256].rearrange("p (a t) -> p a t", a=2))
                                if l == min(2 * lp + 1, 4):
                                    done(ins, "hg_att", s, d, q, lp)
                                    kk_ = jobs[("hg_att", s, d, q, lp)]
                                    dve.wait_ge(free[kk_ % 8], kk_ // 8 + 1)
                                else:
                                    step(ins)
                dve.nop().then_inc(sem("hg_att"), 1)

            def hgrn_out(s):
                if s == 0:
                    dve.wait_ge(sem("hg_after_sb"), 1)
                    tt(hg_att["kh"], hg_att["kh"], hg["kf"], ALU.mult).then_inc(sem("hg_kh"), 1)
                step(tt(hg["gg"], hg["gg"], proj[:, s, HG:HG + 256], ALU.mult))
                b = take(dve, "hg_o", s)
                o, tmp = mix[:, s, 768:1024], hg["fs"][:, 0:256]
                dve.wait_ge(sem("hg_logf"), s + 1)
                step(dve.tensor_copy(o, b[:, 0:256]))
                done(dve.nop(), "hg_o", s)
                step(tt(tmp, o, o, ALU.mult))
                step(dve.tensor_reduce(small8[:, 0:4], by_head(tmp), AX.X, ALU.add))
                rstd(small8[:, 4:8], small8[:, 0:4], 1.0 / DH, EPS)
                step(tt(by_head(o), by_head(o), bc(small8[:, 4:8], [P, 4, DH], 2), ALU.mult))
                step(tt(by_head(o), by_head(o), bc(Pm("hg_g"), [P, 4, DH], 1), ALU.mult))
                step(tt(o, o, hg["gg"], ALU.mult))

            for s in range(2):
                rwkv_keys(s)
                hgrn_rows(s)
                rwkv_rows(s)
                hgrn_pairs(s)
                rwkv_pairs(s)
                hgrn_out(s)
                rwkv_solve(s)
                end_phase(dve, PH_MIX + s)

            for s in range(2):
                nk = 1 + s
                src = proj[:, s, 0:640]
                step(tt(at["sq"], src, src, ALU.mult))
                rs = sel_e["c"][:, 0:10]
                step(dve.tensor_reduce(rs, by_head(at["sq"], 10), AX.X, ALU.add))
                rstd(rs, rs, 1.0 / DH, EPS)
                qn = at["qn"]
                if s:
                    dve.wait_ge(sem("cache_out"), 32)
                tt(qn[:, 0:512].rearrange("p (i g d) -> p g i d", g=2, i=4), src[:, 0:512].rearrange("p (g i d) -> p g i d", g=2, i=4),
                   bc(rs[:, 0:8].rearrange("p (g i) -> p g i", g=2), [P, 2, 4, DH], 3), ALU.mult)
                step(tt(by_head(qn[:, 512:640], 2), by_head(src[:, 512:640], 2), bc(rs[:, 8:10], [P, 2, DH], 2), ALU.mult))
                tt(by_head(qn[:, 0:512], 8), by_head(qn[:, 0:512], 8), bc(Pm("q_g"), [P, 8, DH], 1), ALU.mult)
                step(tt(by_head(qn[:, 512:640], 2), by_head(qn[:, 512:640], 2), bc(Pm("k_g"), [P, 2, DH], 1), ALU.mult))
                if s == 0:
                    dve.nop().then_inc(sem("at_keys"), 1)
                else:
                    pairs = [P, 10, 32]
                    x1, x2 = (qn.rearrange("p (h i e) -> p h i e", h=10, e=2)[:, :, :, e] for e in range(2))
                    r1, r2 = (at["rope"].rearrange("p (h i e) -> p h i e", h=10, e=2)[:, :, :, e] for e in range(2))
                    cos, sin = bc(C("cos"), pairs, 1), bc(C("sin"), pairs, 1)
                    u = [at[n].rearrange("p (h i) -> p h i", h=10) for n in ("t1", "t2", "t3", "t4")]
                    tt(u[0], x1, cos, ALU.mult)
                    tt(u[1], x2, sin, ALU.mult)
                    tt(u[2], x1, sin, ALU.mult)
                    step(tt(u[3], x2, cos, ALU.mult))
                    tt(r1, u[0], u[1], ALU.subtract)
                    step(tt(r2, u[2], u[3], ALU.add))
                dve.nop().then_inc(sem("at_qk"), 1)
                nh = 4 // nk
                mx = sel_e["m8"]
                for i in range(2 * nk):
                    b = take(dve, "at_S", s, i)
                    Sv = b[:, :].rearrange("p (h k) -> p h k", h=nh)
                    step(dve.tensor_reduce(mx[:, 0:nh], Sv, AX.X, ALU.max))
                    tt(at["S"][:, 512 * i:512 * i + 512].rearrange("p (h k) -> p h k", h=nh), Sv,
                       bc(mx[:, 0:nh], [P, nh, P * nk], 2), ALU.subtract).then_inc(sem("at_shift"), 1)
                    dve.wait_ge(sem("at_shift"), (2 if s else 0) + i + 1)
                    done(dve.nop(), "at_S", s, i)
                sums = sel_e["idxf"]
                for i in range(2 * nk):
                    dve.wait_ge(sem("at_P"), (2 if s else 0) + i + 1)
                    step(dve.tensor_reduce(sums[:, nh * i:nh * i + nh],
                                           at["S"][:, 512 * i:512 * i + 512].rearrange("p (h k) -> p h k", h=nh), AX.X, ALU.add))
                step(dve.reciprocal(sums[:, 0:8], sums[:, 0:8]))
                b = take(dve, "at_o", s)
                step(tt(by_head(mix[:, s, 0:512], 8), by_head(b[:, :], 8), bc(sums[:, 0:8], [P, 8, DH], 2), ALU.mult))
                done(dve.nop(), "at_o", s)
                end_phase(dve, PH_AT + s)

            for s in range(2):
                for half in range(2):
                    o = slice(512 * half, 512 * half + 512)
                    b = take(dve, "out", s, half)
                    step(tt(gate1[:, s, o], gate1[:, s, o], b[:, :], ALU.mult))
                    done(dve.nop(), "out", s, half)
            for s in range(2):
                tt(x[:, s, :], x[:, s, :], gate1[:, s, :], ALU.add).then_inc(sem("x2"), 1)
            dve.wait_ge(sem("x2"), 2)
            end_phase(dve, PH_MID)
            sc = scale2
            for s in range(2):
                step(stt(out=sc[:, s, :], in0=sc[:, s, :], scalar=1.0, in1=Pm("ffn_g"), op0=ALU.add, op1=ALU.mult))
            dve.wait_ge(sem("x2_sq"), 2)
            rstd(sel_e["b"][:, 2:4], sel_e["b"][:, 0:2], 1.0 / D, EPS)
            for s in range(2):
                step(stt(out=sc[:, s, :], in0=x[:, s, :], scalar=sel_e["b"][:, 2 + s:3 + s], in1=sc[:, s, :],
                         op0=ALU.mult, op1=ALU.mult))
                tt(h[:, s, :], sc[:, s, :], h[:, s, :], ALU.add).then_inc(sem("h2"), 1)
            b = take(dve, "router")
            dve.wait_ge(sem("h2"), 2)
            lg = sel_e["pos"].rearrange("p (s e) -> p s e", s=2)
            step(tt(lg, b[:, 0:2 * NE].rearrange("p (s e) -> p s e", s=2), bc(Pm("router_b"), [P, 2, NE], 1), ALU.add))
            done(dve.nop(), "router")
            m8 = sel_e["m8"].rearrange("p (s k) -> p s k", s=2)
            for s in range(2):
                dve.max(m8[:, s, :], lg[:, s, :]).then_inc(sem("max8"), 1)
            dve.wait_ge(sem("max8"), 2)
            for s in range(2):
                dve.max_index(idx8[:, s, :], m8[:, s, :], lg[:, s, :]).then_inc(sem("index8"), 1)
            dve.wait_ge(sem("index8"), 2)
            e4 = sel_e["e4"].rearrange("p (s k) -> p s k", s=2)
            step(tt(e4, m8[:, :, 0:4], m8[:, :, 0:1].to_broadcast([P, 2, 4]), ALU.subtract))
            dve.nop().then_inc(sem("shifted"), 1)
            idxf = sel_e["idxf"].rearrange("p (s k) -> p s k", s=2)
            step(dve.tensor_copy(idxf, idx8[:, :, 0:4]))
            dve.wait_ge(free[jobs[("router",)] % 8], 1)
            full4 = [P, 2, TOPK, NE]
            for s in range(2):
                tt(one8[:, s], bc(C("iota_e"), [P, TOPK, NE], 1), bc(idxf[:, s], [P, TOPK, NE], 2), ALU.is_equal) \
                    .then_inc(sem("one_hot"), 1)
            dve.wait_ge(sem("one_hot"), 2)
            for s in range(2):
                dve.tensor_reduce(selm[:, s, :], one8[:, s].rearrange("p k e -> p e k"), AX.X, ALU.add)
            dve.drain().then_inc(sem("chosen"), 1)
            dve.wait_ge(sem("exp4"), 1)
            ssum = sel_e["a"][:, 4:6]
            step(dve.tensor_reduce(ssum, e4, AX.X, ALU.add))
            step(dve.reciprocal(ssum, ssum))
            step(tt(e4, e4, bc(ssum, [P, 2, TOPK], 2), ALU.mult))
            for s in range(2):
                step(tt(tmp_e[:, s], one8[:, s], bc(e4[:, s], [P, TOPK, NE], 2), ALU.mult))
            for s in range(2):
                step(dve.tensor_reduce(gate[:, s, :], tmp_e[:, s].rearrange("p k e -> p e k"), AX.X, ALU.add))
            b = take(dve, "pos")
            step(stt(out=pos, in0=selm, scalar=-1e4, in1=b[:, 0:2 * NE].rearrange("p (s e) -> p s e", s=2),
                     op0=ALU.mult, op1=ALU.add))
            step(ts(pos, pos, 1e4, None, ALU.add))
            step(dve.tensor_reduce(sel_e["cnt"], b[:, 2 * NE:3 * NE], AX.X, ALU.max))
            step(dve.tensor_copy(count_i[:, :], sel_e["cnt"]))
            dve.nop().then_inc(sem("counted"), 1)
            end_phase(dve, PH_ROUTE)

            dve.memset(moe["zero"], 0.0)
            dve.memset(moe["y"], 0.0).then_inc(sem("y_sb"), 1)
            dve.memset(moe["scat"], 0.0).then_inc(sem("scat_sb"), 1)
            dve.drain().then_inc(sem("moe_init"), 1)

            def cut(ap, at_, n):
                return ap[:, at_:at_ + n] if isinstance(at_, int) else ap[:, bass.ds(at_, n)]

            def one_hot(e, b):
                for s in range(2):
                    ins = ts(moe["hot"][:, CAP * s:CAP * s + CAP], cut(C("iota"), b * P, CAP), cut(pos[:, s, :], e, 1), None,
                             ALU.is_equal)
                ins.then_inc(sem("hot_ready"), 1)

            def one_hot_gated(e, b):
                for s in range(2):
                    ins = ts(moe["hotg"][:, P * s:P * s + P], cut(C("iota"), b * P, P), cut(pos[:, s, :], e, 1),
                             cut(gate[:, s, :], e, 1), ALU.is_equal, ALU.mult)
                ins.then_inc(sem("hotg_ready"), 1)

            def expert(n, e, b, e_next, b_next):
                dve.wait_ge(sem("xe_full"), n + 1)
                one_hot(e_next, b_next)
                one_hot_gated(e, b)
                dve.wait_ge(sem("gu_full"), n + 1)
                ts(moe["glu"], bank[4][:, :], LIMIT, None, ALU.min).then_inc(sem("glu_sb"), 1)
                ts(moe["lin"], bank[5][:, :], LIMIT, -LIMIT, ALU.min, ALU.max).then_inc(sem("lin_read"), 1)
                dve.wait_ge(sem("lin_read"), n + 1)
                stt(out=moe["lin"], in0=moe["lin"], scalar=1.0, in1=moe["glu"], op0=ALU.add, op1=ALU.mult) \
                    .then_inc(sem("lin_glu"), 1)
                dve.wait_ge(sem("lin_glu"), n + 1)
                dve.wait_ge(sem("sig_sb"), n + 1)
                tt(moe["act"], moe["lin"], moe["sig"], ALU.mult).then_inc(sem("act_ready"), 1)
                dve.wait_ge(sem("actT_full"), n + 1)
                dve.tensor_copy(moe["actT"], bank[6][:, :]).then_inc(sem("actT_sb"), 1)
                dve.wait_ge(sem("down_full"), n + 1)
                dve.wait_ge(sem("scattered"), n + 1)
                dve.tensor_copy(moe["y"], bank[6][:, :]).then_inc(sem("y_sb"), 1)

            one_hot(0, 0)
            with dve.Fori(0, NE - 1) as e:
                expert(e, e, 0, e + 1, 0)
            expert(NE - 1, NE - 1, 0, 0, 1)
            need = dve.value_load(count_i[0:1, 0:1])
            with dve.If(need > CAP):
                with dve.Fori(1, NBATCH) as bt:
                    with dve.Fori(0, NE - 1) as e:
                        expert(bt * NE + e, e, bt, e + 1, bt)
                    expert(bt * NE + NE - 1, NE - 1, bt, 0, bt + 1)
            dve.drain().then_inc(sem("last_y"), 1)

            dve.wait_ge(sem("acc_full"), 1)
            for s in range(2):
                for half in range(2):
                    cols = slice(512 * half, 512 * half + 512)
                    step(tt(gate2[:, s, cols], gate2[:, s, cols], bank[2 * s + half][:, :], ALU.mult))
                tt(x[:, s, :], x[:, s, :], gate2[:, s, :], ALU.add).then_inc(sem("x3"), 1)
            dve.wait_ge(sem("x3_sq"), 2)
            rstd(sel_e["c"][:, 2:4], sel_e["c"][:, 0:2], 1.0 / D, EPS)
            for s in range(2):
                stt(out=h[:, s, :], in0=x[:, s, :], scalar=sel_e["c"][:, 2 + s:3 + s], in1=Pm("fin_g"),
                    op0=ALU.mult, op1=ALU.mult).then_inc(sem("y_ready"), 1)


_INS = ['x_prompt', 'x_sample', 'cache_att_k', 'cache_att_v', 'state_rwkv', 'state_hgrn', 'c', 'c_ctx',
        'w_mod', 'b_mod', 'norm_mix_g', 'norm_ffn_g', 'w_in', 'w_out', 'att_qnorm_g', 'att_knorm_g',
        'rw_w0', 'rw_w2', 'rw_a0', 'rw_a2', 'rw_g2', 'rw_kk', 'rw_ka', 'rw_rk', 'rw_gn_g', 'rw_gn_b',
        'hg_lb', 'hg_norm_g', 'router_w', 'router_b', 'moe_w_gu', 'moe_b_gu', 'moe_w_down', 'moe_b_down', 'final_norm_g']
_OUTS = [('y_prompt', (1, 128, 1024)), ('y_sample', (1, 128, 1024)), ('new_att_k', (1, 1, 2, 128, 64)),
         ('new_att_v', (1, 1, 2, 128, 64)), ('new_state_rwkv', (1, 1, 2, 4, 64, 64)), ('new_state_hgrn', (1, 1, 2, 4, 64, 64))]


def kernel(**inputs):
    import numpy as _np
    import concourse.bacc as _bacc
    from concourse import mybir as _mybir
    from concourse.bass_utils import run_bass_kernel_spmd as _run

    nc = _bacc.Bacc("TRN2", target_bir_lowering=False, num_devices=1)
    arrays, aps = {}, {}
    for name in _INS + ["constants"]:
        arr = constants() if name == "constants" else _np.ascontiguousarray(inputs[name])
        arrays[f"in_{name}_dram"] = arr
        aps[name] = nc.dram_tensor(f"in_{name}_dram", arr.shape, _mybir.dt.from_np(arr.dtype), kind="ExternalInput").ap()
    for name, shape in _OUTS:
        aps[name] = nc.dram_tensor(f"out_{name}_dram", shape, _mybir.dt.float32, kind="ExternalOutput").ap()
    build(nc, aps)
    r = _run(nc, [arrays], core_ids=[0])
    return tuple(r.results[0][f"out_{name}_dram"] for name, _ in _OUTS)
```
